# Optimizing a Trainium2 kernel written in Bass

```python
import math
import jax, jax.numpy as jnp
from jax import lax
import numpy as np

D_MODEL = 1024
BATCH = 1
SEQ = 512
DEPTH = 1
DEC_BATCH = 8
DEC_SEQ = 8
PAST_LEN = 4096
PAGE_SIZE = 128

PLE_DIM = 256
MIX_WIDTH = D_MODEL
MLSTM_WIDTH = MIX_WIDTH // 2
MLSTM_HEADS = 4
MLSTM_DH = MLSTM_WIDTH // MLSTM_HEADS
MLSTM_CHUNK = 64
POOL_WIDTH = MIX_WIDTH - MLSTM_WIDTH
POOL_WINDOWS = (2, 4, 8, 16)
POOL_GROUPS = len(POOL_WINDOWS)
POOL_GDIM = POOL_WIDTH // POOL_GROUPS
POOL_BUF = max(POOL_WINDOWS) - 1
IN_COLS = 4 * MLSTM_WIDTH + 2 * MLSTM_HEADS + POOL_WIDTH
N_EXPERTS = 64
TOP_K = 8
N_EXPERT_GROUPS = 8
TOPK_GROUPS = 4
EXPERT_FF = 256
SHARED_FF = 256
ROUTED_SCALE = 2.5
MOE_BLOCK = 1024
NORM_EPS = 1e-6

kernel_name = "hymba_mlstm_pool_moe_ple_step"

def _rmsnorm(x, g):
    xf = x.astype(jnp.float32)
    y = xf * lax.rsqrt(jnp.mean(xf * xf, axis=-1, keepdims=True) + NORM_EPS)
    return (y * g.astype(jnp.float32)).astype(x.dtype)

def _mlstm(q, k, v, i_pre, log_f, C0, n0, m0):
    B, H, T, DH = q.shape
    L = math.gcd(T, MLSTM_CHUNK)
    NC = T // L
    chunk4 = lambda t: t.reshape(B, H, NC, L, DH).transpose(2, 0, 1, 3, 4)
    chunk3 = lambda t: t.reshape(B, H, NC, L).transpose(2, 0, 1, 3)
    causal = jnp.tril(jnp.ones((L, L), dtype=bool))

    def step(carry, xs):
        C, n, m = carry
        qc, kc, vc, ic, fc = xs
        b = jnp.cumsum(fc, axis=-1)
        d = b[..., :, None] - b[..., None, :] + ic[..., None, :]
        d = jnp.where(causal, d, -jnp.inf)
        inter = b + m[..., None]
        m_t = jnp.maximum(inter, jnp.max(d, axis=-1))
        w_inter = jnp.exp(inter - m_t)
        s = jnp.einsum('bhtd,bhsd->bhts', qc, kc) * jnp.exp(d - m_t[..., None])
        num = w_inter[..., None] * jnp.einsum('bhtd,bhde->bhte', qc, C) + jnp.einsum('bhts,bhse->bhte', s, vc)
        nq = w_inter * jnp.einsum('bhtd,bhd->bht', qc, n) + jnp.sum(s, axis=-1)
        h = num / jnp.maximum(jnp.abs(nq), jnp.exp(-m_t))[..., None]
        b_last = b[..., -1]
        ls = b_last[..., None] - b + ic
        m_new = jnp.maximum(b_last + m, jnp.max(ls, axis=-1))
        fw = jnp.exp(b_last + m - m_new)
        iw = jnp.exp(ls - m_new[..., None])
        C_new = fw[..., None, None] * C + jnp.einsum('bhs,bhsd,bhse->bhde', iw, kc, vc)
        n_new = fw[..., None] * n + jnp.einsum('bhs,bhsd->bhd', iw, kc)
        return (C_new, n_new, m_new), h

    (C, n, m), hs = lax.scan(step, (C0, n0, m0),
                             (chunk4(q), chunk4(k), chunk4(v), chunk3(i_pre), chunk3(log_f)))
    h = hs.transpose(1, 0, 3, 2, 4).reshape(B, T, H, DH)
    return h, C, n, m

def _pool_mixer(u, buf, start_pos, w_pool, pool_scale):
    B, T, C = u.shape
    R = POOL_BUF
    ext = jnp.concatenate([buf, u], axis=1)
    cs = jnp.concatenate([jnp.zeros((B, 1, C), jnp.float32), jnp.cumsum(ext, axis=1)], axis=1)
    pos = start_pos + jnp.arange(T, dtype=jnp.int32)
    outs = []
    for g, w in enumerate(POOL_WINDOWS):
        sl = slice(g * POOL_GDIM, (g + 1) * POOL_GDIM)
        win_sum = cs[:, R + 1:R + 1 + T, sl] - cs[:, R + 1 - w:R + 1 - w + T, sl]
        cnt = jnp.minimum(pos + 1, w).astype(jnp.float32)
        outs.append(win_sum / cnt[None, :, None] - u[..., sl])
    pooled = jnp.stack(outs, axis=2)
    mixed = jnp.einsum('btgc,gcd->btgd', pooled, w_pool.astype(jnp.float32)).reshape(B, T, C)
    return mixed * pool_scale.astype(jnp.float32), ext[:, -R:]

def _moe(x, router_w, router_bias, ex_w1, ex_w3, ex_w2, sh_w1, sh_w3, sh_w2):
    N, D = x.shape
    E, G = N_EXPERTS, N_EXPERT_GROUPS
    scores = jax.nn.sigmoid(jnp.einsum('nd,de->ne', x.astype(jnp.float32), router_w.astype(jnp.float32)))
    biased = scores + router_bias.astype(jnp.float32)
    group_score = jnp.sum(lax.top_k(biased.reshape(N, G, E // G), 2)[0], axis=-1)
    _, gidx = lax.top_k(group_score, TOPK_GROUPS)
    gmask = jnp.sum(jax.nn.one_hot(gidx, G, dtype=jnp.float32), axis=1)
    emask = jnp.repeat(gmask, E // G, axis=1)
    _, eidx = lax.top_k(jnp.where(emask > 0, biased, -jnp.inf), TOP_K)
    sel = jnp.take_along_axis(scores, eidx, axis=-1)
    wts = sel / jnp.sum(sel, axis=-1, keepdims=True) * ROUTED_SCALE
    gates = jnp.sum(jax.nn.one_hot(eidx, E, dtype=jnp.float32) * wts[..., None], axis=1).astype(x.dtype)
    blk = math.gcd(N, MOE_BLOCK)

    def block(args):
        xb, gb = args
        hb = jax.nn.silu(jnp.einsum('nd,edf->nef', xb, ex_w1)) * jnp.einsum('nd,edf->nef', xb, ex_w3)
        return jnp.einsum('nef,efd->nd', hb * gb[..., None], ex_w2)

    routed = lax.map(block, (x.reshape(N // blk, blk, D), gates.reshape(N // blk, blk, E))).reshape(N, D)
    shared = jnp.einsum('nf,fd->nd', jax.nn.silu(x @ sh_w1) * (x @ sh_w3), sh_w2)
    return routed + shared

def _layer(x, p, C0, n0, m0, buf0, start_pos, norm_mix_g, w_in, b_igate, b_fgate, head_norm_g,
           w_pool, pool_scale, w_out, norm_ffn_g, router_w, router_bias, ex_w1, ex_w3, ex_w2,
           sh_w1, sh_w3, sh_w2, norm_ple_g, w_ple_gate, w_ple_proj):
    B, T, _ = x.shape
    H, DH, W = MLSTM_HEADS, MLSTM_DH, MLSTM_WIDTH
    f32 = jnp.float32
    h = _rmsnorm(x, norm_mix_g)
    z = jnp.einsum('btd,dc->btc', h, w_in).astype(f32)
    q, k, v, o = (z[..., i * W:(i + 1) * W] for i in range(4))
    g0 = 4 * W
    i_pre = z[..., g0:g0 + H] + b_igate.astype(f32)
    log_f = jax.nn.log_sigmoid(z[..., g0 + H:g0 + 2 * H] + b_fgate.astype(f32))
    u = z[..., g0 + 2 * H:]
    heads = lambda t: t.reshape(B, T, H, DH).transpose(0, 2, 1, 3)
    h_a, C, n, m = _mlstm(heads(q) * DH ** -0.5, heads(k), heads(v),
                          i_pre.transpose(0, 2, 1), log_f.transpose(0, 2, 1),
                          C0.astype(f32), n0.astype(f32), m0.astype(f32))
    h_a = h_a * lax.rsqrt(jnp.mean(h_a * h_a, axis=-1, keepdims=True) + NORM_EPS)
    h_a = h_a.reshape(B, T, W) * head_norm_g.astype(f32) * jax.nn.sigmoid(o)
    h_b, buf = _pool_mixer(u, buf0.astype(f32), start_pos, w_pool, pool_scale)
    mix = jnp.concatenate([h_a, h_b], axis=-1).astype(x.dtype)
    x = x + jnp.einsum('btc,cd->btd', mix, w_out)
    y = _moe(_rmsnorm(x, norm_ffn_g).reshape(B * T, -1), router_w, router_bias,
             ex_w1, ex_w3, ex_w2, sh_w1, sh_w3, sh_w2).reshape(B, T, -1)
    x = x + y
    gate = jax.nn.sigmoid(jnp.einsum('btd,de->bte', _rmsnorm(x, norm_ple_g), w_ple_gate))
    x = x + jnp.einsum('btp,pd->btd', p, w_ple_proj) * gate
    return x, C, n, m, buf

def setup_inputs(seed: int = 0) -> dict:
    key = jax.random.key(seed)
    ks = jax.random.split(key, 32)
    f32 = jnp.float32
    H, DH = MLSTM_HEADS, MLSTM_DH

    def nrm(k, shape, scale):
        return jax.random.normal(k, shape, f32) * scale

    def gain(k, shape):
        return 1.0 + 0.02 * jax.random.normal(k, shape, f32)

    return {
        "x_prompt": nrm(ks[0], (BATCH, SEQ, D_MODEL), 1.0),
        "x_sample": nrm(ks[1], (DEC_BATCH, DEC_SEQ, D_MODEL), 1.0),
        "p_prompt": nrm(ks[2], (DEPTH, BATCH, SEQ, PLE_DIM), 1.0),
        "p_sample": nrm(ks[3], (DEPTH, DEC_BATCH, DEC_SEQ, PLE_DIM), 1.0),
        "state_C": nrm(ks[4], (DEPTH, DEC_BATCH, H, DH, DH), DH ** -0.5),
        "state_n": nrm(ks[5], (DEPTH, DEC_BATCH, H, DH), 1.0),
        "state_m": nrm(ks[6], (DEPTH, DEC_BATCH, H), 1.0),
        "state_pool": nrm(ks[7], (DEPTH, DEC_BATCH, POOL_BUF, POOL_WIDTH), 1.0),
        "norm_mix_g": gain(ks[8], (DEPTH, D_MODEL)),
        "w_in": nrm(ks[9], (DEPTH, D_MODEL, IN_COLS), D_MODEL ** -0.5),
        "b_igate": nrm(ks[10], (DEPTH, H), 0.1),
        "b_fgate": jnp.linspace(3.0, 6.0, H, dtype=f32)[None, :] + nrm(ks[11], (DEPTH, H), 0.1),
        "head_norm_g": gain(ks[12], (DEPTH, MLSTM_WIDTH)),
        "w_pool": nrm(ks[13], (DEPTH, POOL_GROUPS, POOL_GDIM, POOL_GDIM), POOL_GDIM ** -0.5),
        "pool_scale": gain(ks[14], (DEPTH, POOL_WIDTH)),
        "w_out": nrm(ks[15], (DEPTH, MIX_WIDTH, D_MODEL), MIX_WIDTH ** -0.5),
        "norm_ffn_g": gain(ks[16], (DEPTH, D_MODEL)),
        "router_w": nrm(ks[17], (DEPTH, D_MODEL, N_EXPERTS), D_MODEL ** -0.5),
        "router_bias": nrm(ks[18], (DEPTH, N_EXPERTS), 0.01),
        "ex_w1": nrm(ks[19], (DEPTH, N_EXPERTS, D_MODEL, EXPERT_FF), D_MODEL ** -0.5),
        "ex_w3": nrm(ks[20], (DEPTH, N_EXPERTS, D_MODEL, EXPERT_FF), D_MODEL ** -0.5),
        "ex_w2": nrm(ks[21], (DEPTH, N_EXPERTS, EXPERT_FF, D_MODEL), EXPERT_FF ** -0.5),
        "sh_w1": nrm(ks[22], (DEPTH, D_MODEL, SHARED_FF), D_MODEL ** -0.5),
        "sh_w3": nrm(ks[23], (DEPTH, D_MODEL, SHARED_FF), D_MODEL ** -0.5),
        "sh_w2": nrm(ks[24], (DEPTH, SHARED_FF, D_MODEL), SHARED_FF ** -0.5),
        "norm_ple_g": gain(ks[25], (DEPTH, D_MODEL)),
        "w_ple_gate": nrm(ks[26], (DEPTH, D_MODEL, D_MODEL), D_MODEL ** -0.5),
        "w_ple_proj": nrm(ks[27], (DEPTH, PLE_DIM, D_MODEL), PLE_DIM ** -0.5),
        "final_norm_g": gain(ks[28], (D_MODEL,)),
    }

def reference(x_prompt, x_sample, p_prompt, p_sample, state_C, state_n, state_m, state_pool,
              norm_mix_g, w_in, b_igate, b_fgate, head_norm_g, w_pool, pool_scale, w_out,
              norm_ffn_g, router_w, router_bias, ex_w1, ex_w3, ex_w2, sh_w1, sh_w3, sh_w2,
              norm_ple_g, w_ple_gate, w_ple_proj, final_norm_g):
    f32 = jnp.float32
    H, DH = MLSTM_HEADS, MLSTM_DH
    B = x_prompt.shape[0]
    xp, xs = x_prompt, x_sample
    Cp, Np, Mp, Bp = [], [], [], []
    Cs, Ns, Ms, Bs = [], [], [], []
    for l in range(DEPTH):
        lw = (norm_mix_g[l], w_in[l], b_igate[l], b_fgate[l], head_norm_g[l], w_pool[l], pool_scale[l],
              w_out[l], norm_ffn_g[l], router_w[l], router_bias[l], ex_w1[l], ex_w3[l], ex_w2[l],
              sh_w1[l], sh_w3[l], sh_w2[l], norm_ple_g[l], w_ple_gate[l], w_ple_proj[l])
        xp, c, n, m, bf = _layer(xp, p_prompt[l], jnp.zeros((B, H, DH, DH), f32), jnp.zeros((B, H, DH), f32),
                                 jnp.zeros((B, H), f32), jnp.zeros((B, POOL_BUF, POOL_WIDTH), f32), 0, *lw)
        Cp.append(c); Np.append(n); Mp.append(m); Bp.append(bf)
        xs, c, n, m, bf = _layer(xs, p_sample[l], state_C[l], state_n[l], state_m[l], state_pool[l],
                                 PAST_LEN, *lw)
        Cs.append(c); Ns.append(n); Ms.append(m); Bs.append(bf)
    y_prompt = _rmsnorm(xp, final_norm_g)
    y_sample = _rmsnorm(xs, final_norm_g)
    return (y_prompt, y_sample, jnp.stack(Cp), jnp.stack(Np), jnp.stack(Mp), jnp.stack(Bp),
            jnp.stack(Cs), jnp.stack(Ns), jnp.stack(Ms), jnp.stack(Bs))


_drawn_inputs = setup_inputs


def setup_inputs(seed=0):
    import zlib

    import numpy as np

    out = dict(_drawn_inputs(seed))
    spreads = {}
    factors = {'norm_ple_g': 50.325, 'final_norm_g': 7.473}
    for name, (base, spread) in spreads.items():
        noise = np.random.default_rng([zlib.crc32(name.encode()), seed]).standard_normal(out[name].shape)
        drawn = base * np.exp(spread * noise) if base else spread * noise
        out[name] = __import__('jax').numpy.asarray(drawn.astype(out[name].dtype))
    for name, factor in factors.items():
        out[name] = (out[name] * factor).astype(out[name].dtype)
    return out
```

```python
from contextlib import ExitStack

import concourse.bass as bass
from concourse import mybir

F32 = mybir.dt.float32
I32 = mybir.dt.int32
ALU = mybir.AluOpType
ACT = mybir.ActivationFunctionType
AX = mybir.AxisListType

P = 128
EPS = 1e-6
NEG = -1e30
FAR = 100000
ROUTED_SCALE = 2.5
WINDOWS = (2, 4, 8, 16)


def psum_groups(NT, H, KH):
    g = []
    for i in range(NT):
        g += [(("x1T", i, 0), "v"), (("x1T", i, 1), "s")]
    g += [(("g", 0), "v"), (("g", 1), "v")]
    g += [(("q", j, n), "s") for j in range(H) for n in range(2)]
    g += [(("k", j, n), "s") for j in range(H) for n in range(2)]
    g += [(("u", j, n), "v") for j in range(H) for n in range(2)]
    g += [(("buf",), "v")]
    g += [(("v", i), "v") for i in range(NT)]
    g += [(("nat",), "v")]
    g += [(("mix", j, n), "s") for j in range(H) for n in range(2)]
    g += [(("pp",), "s"), (("ps",), "s")]
    for h in range(H):
        g += [(("Mb", h), "v")] + [(("S", h, j), "v") for j in range(4)]
        g += [(("o", h), "s")]
        g += [(("num", h, i), "s") for i in range(4)]
    g += [(("Ms", 0), "v"), (("Ms", 1), "v"), (("Ss",), "v")]
    for h in range(H):
        g += [(("kn", h), "v"), (("Cp", h), "s")]
    g += [(("kns",), "s"), (("n0",), "v"), (("o", 4), "s"), (("nT",), "s"), (("nqs",), "v"), (("nTt",), "s")]
    g += [(("C", h, c), "v") for h in range(H) for c in range(3)]
    g += [(("haT", i), "v") for i in range(NT)]
    g += [(("nout",), "s")]

    def wo(i):
        return [(("wo", i, 0), "v"), (("wo", i, 1), "v")]

    def norm2(i):
        return [(("x2T", i, 0), "v"), (("x2T", i, 1), "s"), (("r", i), "s"), (("sh", i), "v")]

    def shared(i):
        return [(("shT", i), "s"), (("y", i, 0), "v"), (("y", i, 1), "v")]

    g += wo(0) + wo(1) + norm2(0) + wo(2) + shared(0) + norm2(1) + wo(3) + shared(1) + norm2(2)
    g += wo(4) + shared(2) + norm2(3)
    g += [(("pT", i), "s") for i in range(NT)]
    g += shared(3) + norm2(4)
    g += [(("pj", i, n), "s") for i in range(2) for n in range(2)]
    g += shared(4)
    g += [(("pj", i, n), "s") for i in range(2, NT) for n in range(2)]
    g += [(("pos",), "v")]
    for i in range(NT):
        g += [(("x3T", i, 0), "v"), (("x3T", i, 1), "s"), (("gt", i, 0), "s"), (("gt", i, 1), "s")]
    return g


def decoder_step(nc, x_prompt, x_sample, p_prompt, p_sample, state_C, state_n, state_m, state_pool,
                 norm_mix_g, w_in, b_igate, b_fgate, head_norm_g, w_pool, pool_scale, w_out,
                 norm_ffn_g, router_w, router_bias, ex_w1, ex_w3, ex_w2, sh_w1, sh_w3, sh_w2,
                 norm_ple_g, w_ple_gate, w_ple_proj, final_norm_g,
                 y_prompt, y_sample, C_prompt, n_prompt, m_prompt, pool_prompt,
                 C_sample, n_sample, m_sample, pool_sample):
    _, SEQ, DM = x_prompt.shape
    NB, DS, _ = x_sample.shape
    H = state_C.shape[2]
    NE = ex_w1.shape[1]
    FF = ex_w1.shape[3]
    PLE = p_prompt.shape[3]
    R = state_pool.shape[2]
    NP_ = SEQ // P
    NT = NP_ + 1
    NS = NB * DS
    T = SEQ + NS
    TH = T // 2
    KT = DM // P
    MW = H * P
    DE = P + 1
    ROWS = [P] * NP_ + [NS]
    SEGP = R + SEQ
    SEGS = R + DS
    EXT = SEGP + NB * SEGS
    NG = 8
    K = 8
    PASSES = -(-T // P)
    NEX = NE + 2
    assert (SEQ, NS, DM, H, NE, FF, PLE, R) == (512, 64, 1024, 4, 64, 256, 256, 15)
    STORES = 1 + 1 + NB + 2 + 1 + NB + 2
    BLK = [0]
    for j in range(NP_):
        BLK.append(BLK[-1] + SEQ - P * j)

    ctx = ExitStack()
    with ctx:
        def sb(name, shape, dt=F32):
            return ctx.enter_context(nc.sbuf_tensor(name, shape, dt))

        def sem(name):
            return ctx.enter_context(nc.semaphore(name))

        def tok(i):
            return slice(P * i, P * i + ROWS[i])

        xs_dram = nc.dram_tensor("xs_dram", [T, DM], F32).ap()
        ex_dram = nc.dram_tensor("ex_dram", [T * K, DM], F32).ap()

        x = sb("x", [P, NT, DM])
        xT = sb("xT", [P, KT, T])
        mixpj = sb("mixpj", [P, NT * DM])
        mixT = mixpj[:, 0:KT * T].rearrange("p (c t) -> p c t", t=T)
        proj = mixpj[:, :].rearrange("p (i n) -> p i n", n=DM)
        ring = sb("ring", [P, 2, KT * 512])
        g_a = sb("g_a", [P, DM])
        g_b = sb("g_b", [P, DM])
        ident = sb("ident", [P, P])
        tri = sb("tri", [P, P])
        before = sb("before", [P, P])
        onesf = sb("onesf", [P, P])
        iotaf = sb("iotaf", [P, P])
        iotap = sb("iotap", [P, P])
        small = sb("small", [P, 32])
        eps_c, neg_half = small[:, 0:1], small[:, 1:2]
        gate_b = small[:, 2:3]
        hn_g = small[:, 4:8]
        pl_s = small[:, 8:12]
        ss = sb("ss", [P, NT])
        rstd = sb("rstd", [P, NT])
        junk = sb("junk", [P, DM])

        ARENA = 25503
        arena = sb("arena", [P, ARENA])
        used = {"mixer": 0, "experts": 0}

        def carve(phase, n, at=None):
            if at is None:
                at = used[phase]
                used[phase] += n
                assert used[phase] <= ARENA
            return arena[:, at:at + n], at

        def mx(n):
            return carve("mixer", n)[0]

        def ex(n):
            return carve("experts", n)[0]

        def over(at, n):
            return carve("mixer", n, at)[0]

        qT_raw, q_at = carve("mixer", H * T)
        qT = qT_raw.rearrange("p (h t) -> p h t", t=T)
        kT = mx(H * T).rearrange("p (h t) -> p h t", t=T)
        pool_raw, pool_at = carve("mixer", H * EXT + 2 * EXT + 2 * T)
        uext = pool_raw[:, 0:H * EXT].rearrange("p (g t) -> p g t", t=EXT)
        wsum = pool_raw[:, H * EXT:(H + 2) * EXT].rearrange("p (b t) -> p b t", t=EXT)
        pooled = pool_raw[:, (H + 2) * EXT:].rearrange("p (b t) -> p b t", t=T)
        C0 = carve("mixer", NB * H * DE, pool_at)[0].rearrange("p (b h e) -> p b h e", h=H, e=DE)
        c_at = pool_at + NB * H * DE
        D, d_at = carve("mixer", BLK[-1])
        PT, pt_at = carve("mixer", BLK[-1])
        wg = over(pt_at, KT * 36).rearrange("p (c n) -> p c n", n=36)
        bufnat = over(pt_at + 288, MW)[0:NB * R, :]
        iotai = over(pt_at + 800, P).bitcast(I32)
        us = over(pt_at + 992, H * NS).rearrange("p (h t) -> p h t", t=NS)
        Vb = carve("mixer", NB * DE, pt_at)[0].rearrange("p (b e) -> p b e", e=DE)
        v = mx(NT * H * DE).rearrange("p (i h e) -> p i h e", h=H, e=DE)
        so_raw, so_at = carve("mixer", NT * MW)
        so = so_raw.rearrange("p (i n) -> p i n", n=MW)
        xs1 = carve("mixer", 2 * DM, so_at)[0].rearrange("p (b n) -> p b n", n=DM)
        nb_raw, nb_at = carve("mixer", NT * H * DE)
        nb = nb_raw.rearrange("p (i h e) -> p i h e", h=H, e=DE)
        rows4 = [carve("mixer", T, nb_at + k * T)[0][0:H, :] for k in range(4)]
        r_i, r_f, r_e, r_l = rows4
        a_row, M_row, m_row = (mx(T)[0:H, :] for _ in range(3))
        keep = over(d_at, T)[0:H, :]
        reset = over(d_at + T, T)[0:H, :]
        srow = mx(NS + NS + NB)[0:H, :]
        m0row = mx(NB)[0:H, :]
        em_row = mx(T)[0:H, :]
        anat = mx(2 * NT * H).rearrange("p (a i h) -> p a i h", i=NT, h=H)
        wcol = mx(NP_ * H).rearrange("p (j h) -> p j h", h=H)
        fwb = mx(H * NB).rearrange("p (h b) -> p h b", b=NB)
        sel4 = mx(H * P).rearrange("p (h n) -> p h n", n=P)[0:H]
        bd = mx(NS)[0:NS, :]
        bmask = mx(NB + 1)[0:NS, :]
        rcnt = mx(H * 16).rearrange("p (g n) -> p g n", n=16)
        rcnt_i = mx(H * 16).bitcast(I32).rearrange("p (g n) -> p g n", n=16)
        kw = over(d_at, 2 * MW).rearrange("p (b j d) -> p b j d", j=NP_, d=P)
        kws = over(c_at, MW).rearrange("p (h d) -> p h d", d=P)[0:NS]
        wp_raw, wp_at = carve("mixer", H * P)
        wp = wp_raw.rearrange("p (g d) -> p g d", d=P)
        Ds = over(wp_at, H * NS).rearrange("p (h t) -> p h t", t=NS)[0:NS]
        PTs = over(wp_at + H * NS, H * NS).rearrange("p (h t) -> p h t", t=NS)[0:NS]
        qw = mx(H * NS).rearrange("p (h t) -> p h t", t=NS)
        numT = over(c_at + MW, H * NS).rearrange("p (h t) -> p h t", t=NS)
        nq9 = mx(H * (NB + 1)).rearrange("p (h c) -> p h c", c=NB + 1)[0:NS]
        Cp = over(q_at + 2 * MW, H * DE).rearrange("p (h e) -> p h e", e=DE)
        n0nat = over(c_at + MW + H * NS, P)[0:NB * H, :]
        nout = over(c_at + MW + H * NS + P, 2 * P)[0:NB * H, :]
        ppo = mx(MW)[0:R, :]
        pso = mx(MW)[0:NS, :]
        fac = mx(6 * NT * H).rearrange("p (k i h) -> p k i h", i=NT, h=H)
        ha = over(q_at, 2 * MW).rearrange("p (b n) -> p b n", n=MW)

        w13, w2s = [], []
        for _ in range(2):
            w13.append(ex(2 * KT * FF).rearrange("p (w c f) -> p w c f", w=2, f=FF))
            w2s.append(ex(2 * DM).rearrange("p (c n) -> p c n", n=DM))
        xg = [ex(DM) for _ in range(2)]
        xgT = [ex(DM).rearrange("p (c t) -> p c t", t=P) for _ in range(2)]
        og_at = used["experts"]
        og = [ex(DM) for _ in range(2)]
        onehot = [ex(NT * P).rearrange("p (i t) -> p i t", t=P) for _ in range(2)]
        hs = ex(FF)
        hh = ex(FF)
        hT = ex(2 * P).rearrange("p (c t) -> p c t", t=P)
        NC = 4 * NT
        table = ex((NEX + 3) * NC).rearrange("p (e c) -> p e c", c=NC)
        cols = [ex(NC) for _ in range(2)]
        sc_, bi_, t1_, t2_, sel_, gt_ = (ex(NT * NE).rearrange("p (i e) -> p i e", e=NE) for _ in range(6))
        gs_ = ex(8 * NT * NG).rearrange("p (k i g) -> p k i g", i=NT, g=NG)
        rbias = ex(NE)
        rw = arena[:, og_at:og_at + KT * NE].rearrange("p (c e) -> p c e", e=NE)
        p_at = og_at + KT * NE
        ptile = arena[:, p_at:p_at + NT * PLE].rearrange("p (i n) -> p i n", n=PLE)
        pT = arena[:, p_at + NT * PLE:p_at + NT * PLE + 2 * T].rearrange("p (c t) -> p c t", t=T)
        lower = ex(NG * NG).rearrange("p (a b) -> p a b", b=NG)
        top = ex(NT * K).rearrange("p (i k) -> p i k", k=K)
        keys = ex(NT * K).rearrange("p (i k) -> p i k", k=K)
        xs2 = xg
        xs3 = [a.rearrange("p c t -> p (c t)") for a in xgT]
        cg = [arena[:, k * DM:(k + 1) * DM] for k in range(K)]
        gsig = [arena[:, (K + k) * DM:(K + k + 1) * DM] for k in range(2)]
        tokf = sb("tokf", [P, NT])
        toki = sb("toki", [P, NT], I32)
        ebase = sb("ebase", [P, NE])
        keyi = sb("keyi", [P, NT, K], I32)
        slot = [sb(f"slot{k}", [P, 2], I32) for k in range(4)]
        gate = [sb(f"gate{k}", [P, 1]) for k in range(4)]
        np_f = sb("np_f", [1, 4])
        np_i = sb("np_i", [1, 1], I32)

        bank = [ctx.enter_context(nc.psum_tensor(f"bank{k}", [P, 512], F32)) for k in range(8)]

        s_x = [sem(f"s_xin{i}") for i in range(NT)]
        s_small = sem("s_small")
        s_ga, s_gb = sem("s_ga"), sem("s_gb")
        s_ring = [sem("s_ring0"), sem("s_ring1")]
        s_wg = sem("s_wg")
        s_state = sem("s_state")
        s_c0 = sem("s_c0")
        s_const = sem("s_const")
        filled = sem("filled")
        drained = {"v": sem("drained_v"), "s": sem("drained_s")}
        s_sq = sem("s_sq")
        s_rstd = sem("s_rstd")
        s_xs = sem("s_xs")
        s_abs, s_ln, s_mrow, s_em = sem("s_abs"), sem("s_ln"), sem("s_mrow"), sem("s_em")
        s_wsum, s_pooled = sem("s_wsum"), sem("s_pooled")
        s_dif, s_exp, s_msk, s_pt = sem("s_dif"), sem("s_exp"), sem("s_msk"), sem("s_pt")
        s_difs, s_exps, s_msks, s_vb, s_place = (sem(n) for n in ("s_difs", "s_exps", "s_msks", "s_vb", "s_place"))
        s_sqh, s_var, s_pw, s_ha = sem("s_sqh"), sem("s_var"), sem("s_pw"), sem("s_ha")
        s_stat = sem("s_stat")
        s_sh, s_p, s_rt = sem("s_sh"), sem("s_p"), sem("s_rt")
        s_x1 = sem("s_x1")
        s_silu_sh, s_hsh = sem("s_silu_sh"), sem("s_hsh")
        s_xsd = [sem("s_xsd0"), sem("s_xsd1")]
        s_sel0 = sem("s_sel0")
        s_np = sem("s_np")
        s_carried = sem("s_carried")
        s_w13 = [sem("s_w13a"), sem("s_w13b")]
        s_w2 = [sem("s_w2a"), sem("s_w2b")]
        s_gather = [sem("s_gather0"), sem("s_gather1")]
        s_scatter = [sem("s_scatter0"), sem("s_scatter1")]
        (s_cols, s_onehot, s_index, s_h, s_xgT0, s_out1, s_silu, s_xgT1, s_hT, s_out0,
         s_psel, s_pxt, s_mm1, s_pht, s_mm2) = (sem(n) for n in (
             "s_cols", "s_onehot", "s_index", "s_h", "s_xgT0", "s_out1", "s_silu", "s_xgT1", "s_hT", "s_out0",
             "s_psel", "s_pxt", "s_mm1", "s_pht", "s_mm2"))
        s_cg = [sem(f"s_cg{k}") for k in range(K)]
        s_x2 = sem("s_x2")
        s_x3, s_y = sem("s_x3"), sem("s_y")
        s_yo = [sem("s_yo0"), sem("s_yo1")]
        dve_step, act_step, pool_step = sem("dve_step"), sem("act_step"), sem("pool_step")

        GROUPS = psum_groups(NT, H, KT)
        AT = {key: n for n, (key, _) in enumerate(GROUPS)}
        ORD, seen = {}, {"v": 0, "s": 0}
        for key, e in GROUPS:
            seen[e] += 1
            ORD[key] = (e, seen[e])

        def free_bank(pe, *key):
            g = AT[key]
            if g >= 8:
                e, n = ORD[GROUPS[g - 8][0]]
                pe.wait_ge(drained[e], n)
            return bank[g % 8]

        def full_bank(eng, *key):
            eng.wait_ge(filled, AT[key] + 1)
            return bank[AT[key] % 8]

        def after(eng, *key):
            eng.wait_ge(filled, AT[key] + 1)

        def wait_drained(eng, *key):
            e, n = ORD[key]
            eng.wait_ge(drained[e], n)

        progress = {"v": 0, "s": 0}

        def drain(e, ins, *key):
            progress[e] += 1
            assert ORD[key] == (e, progress[e]), (key, ORD[key], progress[e])
            ins.then_inc(drained[e], 1)

        CH = ["q", "k", "u", "v", "o", "wo0", "wo1", "pj", "gt0", "gt1"]
        wcol0 = {"q": 0, "k": MW, "v": 2 * MW, "o": 3 * MW, "u": 4 * MW + 2 * H}
        LAST = {"q": ("q", 3, 1), "k": ("k", 3, 1), "u": ("u", 3, 1), "v": ("v", 4), "o": ("o", 4),
                "wo0": ("wo", 4, 0), "wo1": ("wo", 4, 1), "pj": ("pj", 4, 1)}

        def chunk(name):
            return ring[:, CH.index(name) % 2, :]

        def chunk_in(eng, name):
            c = CH.index(name)
            eng.wait_ge(s_ring[c % 2], 16 * (c // 2 + 1))

        def bc(dram_row, n=P):
            return dram_row.partition_broadcast(n)

        HG = NEX // 2 * 16
        block = ctx.enter_context(nc.Block())

        @block.sync
        def _(sp):
            xin = [x_prompt[0, P * i:P * i + P, :] for i in range(NP_)] + [x_sample.rearrange("b t d -> (b t) d")]
            sp.dma_start(x[:, 0, :], xin[0]).then_inc(s_x[0], 16)
            sp.dma_start(g_a[:, :], bc(norm_mix_g[0])).then_inc(s_ga, 16)
            for i in range(1, NT):
                sp.dma_start(x[0:ROWS[i], i, :], xin[i]).then_inc(s_x[i], 16)
            wi = w_in[0].rearrange("(p c) n -> p c n", c=KT)
            sp.wait_ge(s_const, 1)
            sp.dma_start(wg[:, :, 0:H], wi[:, :, 4 * MW:4 * MW + H]).then_inc(s_wg, 16)
            sp.dma_start(wg[:, :, 32:32 + H], wi[:, :, 4 * MW + H:4 * MW + 2 * H]).then_inc(s_wg, 16)

            def load_chunk(name):
                c = CH.index(name)
                if c >= 2:
                    after(sp, *LAST[CH[c - 2]])
                if name in wcol0:
                    n0 = wcol0[name]
                    dst, src = chunk(name).rearrange("p (c n) -> p c n", n=512), wi[:, :, n0:n0 + 512]
                elif name[:2] == "wo":
                    n0 = 512 * int(name[2])
                    dst = chunk(name).rearrange("p (c n) -> p c n", n=512)
                    src = w_out[0].rearrange("(c p) n -> p c n", p=P)[:, :, n0:n0 + 512]
                elif name == "pj":
                    dst = chunk(name)[:, 0:2 * DM].rearrange("p (c n) -> p c n", n=DM)
                    src = w_ple_proj[0].rearrange("(c p) n -> p c n", p=P)
                else:
                    n0 = 512 * int(name[2])
                    dst = chunk(name).rearrange("p (c n) -> p c n", n=512)
                    src = w_ple_gate[0].rearrange("(p c) n -> p c n", c=KT)[:, :, n0:n0 + 512]
                sp.dma_start(dst, src).then_inc(s_ring[c % 2], 16)

            load_chunk("q")
            sp.dma_start(gate_b[0:H, :], b_igate.rearrange("a h -> h a"),
                         allow_slow_non_contiguous=True).then_inc(s_small, 16)
            sp.dma_start(gate_b[32:32 + H, :], b_fgate.rearrange("a h -> h a"),
                         allow_slow_non_contiguous=True).then_inc(s_small, 16)
            sp.dma_start(hn_g, head_norm_g[0].rearrange("(h p) -> p h", p=P),
                         allow_slow_non_contiguous=True).then_inc(s_small, 16)
            sp.dma_start(pl_s, pool_scale[0].rearrange("(h p) -> p h", p=P),
                         allow_slow_non_contiguous=True).then_inc(s_small, 16)
            sp.dma_start(m0row, state_m[0].rearrange("b h -> h b"),
                         allow_slow_non_contiguous=True).then_inc(s_small, 16)
            load_chunk("k")
            sp.dma_start(g_b[:, :], bc(norm_ffn_g[0])).then_inc(s_gb, 16)
            sp.dma_start(bufnat, state_pool[0].rearrange("b r c -> (b r) c")).then_inc(s_state, 16)
            sp.dma_start(wp, w_pool[0].rearrange("g c d -> c g d")).then_inc(s_state, 16)
            sp.dma_start(pool_sample[0, :, 0:R - DS, :], state_pool[0, :, DS:R, :]).then_inc(s_stat, 16)
            load_chunk("u")
            load_chunk("v")
            load_chunk("o")
            after(sp, "ps")
            after(sp, "mix", 3, 1)
            for b in range(NB):
                sp.dma_start(C0[:, b, :, 0:P], state_C[0, b].rearrange("h d e -> d h e")).then_inc(s_c0, 16)
            sp.dma_start(n0nat, state_n[0].rearrange("b h d -> (b h) d")).then_inc(s_c0, 16)
            wait_drained(sp, "ps")
            sp.dma_start(pool_prompt[0, 0], ppo).then_inc(s_stat, 16)
            for b in range(NB):
                sp.dma_start(pool_sample[0, b, R - DS:R, :], pso[DS * b:DS * b + DS, :]).then_inc(s_stat, 16)
            load_chunk("wo0")
            load_chunk("wo1")
            sp.dma_start(m_prompt[0].rearrange("a h -> h a"), m_row[:, SEQ - 1:SEQ],
                         allow_slow_non_contiguous=True).then_inc(s_stat, 16)
            sp.dma_start(m_sample[0].rearrange("b h -> h b"), m_row[:, SEQ + DS - 1:T:DS],
                         allow_slow_non_contiguous=True).then_inc(s_stat, 16)
            wait_drained(sp, "Cp", 3)
            sp.dma_start(C_prompt[0, 0].rearrange("h d e -> d h e"), Cp[:, :, 0:P]).then_inc(s_stat, 16)
            wait_drained(sp, "C", 3, 2)
            for b in range(NB):
                sp.dma_start(C_sample[0, b].rearrange("h d e -> d h e"), C0[:, b, :, 0:P]).then_inc(s_stat, 16)
            wait_drained(sp, "nout")
            sp.dma_start(n_sample[0].rearrange("b h d -> (b h) d"), nout[:, 0:P]).then_inc(s_stat, 16)
            sp.dma_start(n_prompt[0, 0], nout[0:H, P:2 * P]).then_inc(s_stat, 16)
            sp.wait_ge(s_stat, 16 * STORES)
            wait_drained(sp, "haT", NT - 1)
            sp.dma_start(rw, router_w[0].rearrange("(p c) e -> p c e", c=KT)).then_inc(s_rt, 16)
            sp.dma_start(rbias, bc(router_bias[0])).then_inc(s_rt, 16)

            def load_expert(j, w1, w3, w2, s13, s2):
                sp.dma_start(w13[j][:, 0], w1.rearrange("(p c) f -> p c f", c=KT)).then_inc(s13, 16)
                sp.dma_start(w13[j][:, 1], w3.rearrange("(p c) f -> p c f", c=KT)).then_inc(s13, 16)
                sp.dma_start(w2s[j], w2.rearrange("(c p) n -> p c n", p=P)).then_inc(s2, 16)

            load_expert(1, sh_w1[0], sh_w3[0], sh_w2[0], s_sh, s_sh)
            for i in range(NP_):
                sp.dma_start(ptile[:, i, :], p_prompt[0, 0, P * i:P * i + P, :]).then_inc(s_p, 16)
            sp.dma_start(ptile[0:NS, NP_, :], p_sample[0].rearrange("b t n -> (b t) n")).then_inc(s_p, 16)
            load_expert(0, ex_w1[0, 0], ex_w3[0, 0], ex_w2[0, 0], s_w13[0], s_w2[0])
            sp.wait_ge(s_xs, NT)
            sp.dma_start(g_a[:, :], bc(norm_ple_g[0])).then_inc(s_ga, 16)
            for i in range(NT):
                if i == NT - 1:
                    load_chunk("pj")
                sp.wait_ge(s_xs, NT + i + 1)
                sp.dma_start(xs_dram[P * i:P * i + ROWS[i], :], xs2[i % 2][0:ROWS[i], :]).then_inc(s_xsd[i % 2], 16)
            sp.dma_start(g_b[:, :], bc(final_norm_g)).then_inc(s_gb, 16)
            load_chunk("gt0")
            after(sp, "y", NT - 1, 1)
            load_expert(1, ex_w1[0, 1], ex_w3[0, 1], ex_w2[0, 1], s_w13[1], s_w2[1])
            load_chunk("gt1")
            sp.wait_ge(s_np, 1)
            passes = sp.value_load(np_i[0:1, 0:1], min_val=1, max_val=PASSES)
            with sp.Fori(2, passes * NE, 2) as n:
                for j in range(2):
                    e = sp.snap((n + j) % NE)
                    sp.wait_ge(s_mm1, n + j - 1)
                    sp.dma_start(w13[j][:, 0], ex_w1[0, bass.ds(e, 1)].rearrange("a (p c) f -> p (a c) f", c=KT)
                                 ).then_inc(s_w13[j], 16)
                    sp.dma_start(w13[j][:, 1], ex_w3[0, bass.ds(e, 1)].rearrange("a (p c) f -> p (a c) f", c=KT)
                                 ).then_inc(s_w13[j], 16)
                    sp.wait_ge(s_mm2, n + j - 1)
                    sp.dma_start(w2s[j], ex_w2[0, bass.ds(e, 1)].rearrange("a (c p) n -> p (a c) n", p=P)
                                 ).then_inc(s_w2[j], 16)
            yout = [y_prompt[0, P * i:P * i + P, :] for i in range(NP_)] + [y_sample.rearrange("b t d -> (b t) d")]
            for i in range(NT):
                sp.wait_ge(s_y, i + 1)
                sp.dma_start(yout[i], og[i % 2][0:ROWS[i], :]).then_inc(s_yo[i % 2], 16)
            sp.wait_ge(s_yo[0], 16 * 3)
            sp.wait_ge(s_yo[1], 16 * 2)

        @block.gpsimd
        def _(pool):
            n_step = [0]

            def link(ins):
                n_step[0] += 1
                ins.then_inc(pool_step, 1)
                pool.wait_ge(pool_step, n_step[0])

            pool.memset(wg, 0.0).then_inc(s_const, 1)
            pool.memset(eps_c, EPS)
            pool.memset(neg_half, -0.5)
            pool.memset(onesf[:, :], 1.0)
            pool.memset(tri[:, :], 1.0)
            pool.memset(before[:, :], 1.0)
            pool.memset(sel4, 0.0)
            pool.memset(bmask, 1.0)
            pool.memset(keep, 1.0)
            pool.memset(reset, 0.0)
            link(pool.memset(ident[:, :], 0.0))
            pool.affine_select(out=ident[:, :], in_=ident[:, :], compare_op=ALU.not_equal, fill=1.0, base=0,
                               pattern=[[-1, P]], channel_multiplier=1).then_inc(s_const, 1)
            pool.memset(keep[:, SEQ:T:DS], 0.0)
            pool.memset(reset[:, SEQ:T:DS], NEG)
            pool.memset(v[:, :, :, P:DE], 1.0)
            pool.memset(uext[:, :, 0:R], 0.0)
            pool.affine_select(out=tri[:, :], in_=tri[:, :], compare_op=ALU.is_ge, fill=0.0, base=0,
                               pattern=[[1, P]], channel_multiplier=-1)
            pool.affine_select(out=before[:, :], in_=before[:, :], compare_op=ALU.is_ge, fill=0.0, base=-1,
                               pattern=[[1, P]], channel_multiplier=-1)
            pool.affine_select(out=sel4, in_=sel4, compare_op=ALU.not_equal, fill=1.0, base=0,
                               pattern=[[-1, H], [0, P]], channel_multiplier=1)
            link(pool.affine_select(out=bmask[:, 0:NB], in_=bmask[:, 0:NB], compare_op=ALU.is_ge, fill=0.0, base=0,
                                    pattern=[[-DS, NB]], channel_multiplier=1))
            pool.affine_select(out=bmask[:, 0:NB], in_=bmask[:, 0:NB], compare_op=ALU.is_ge, fill=0.0, base=DS - 1,
                               pattern=[[DS, NB]], channel_multiplier=-1)
            bd3 = bd.rearrange("p (b t) -> p b t", t=DS)
            pool.affine_select(out=bd3, in_=tri[0:NS, 0:NS].rearrange("p (b t) -> p b t", t=DS),
                               compare_op=ALU.is_ge, fill=0.0, base=0, pattern=[[-DS, NB], [0, DS]],
                               channel_multiplier=1)
            pool.iota(rcnt_i, pattern=[[0, H], [1, 16]], base=1, channel_multiplier=0)
            pool.iota(toki[:, :], pattern=[[P, NT]], base=-FAR, channel_multiplier=1)
            link(pool.iota(iotai, pattern=[[1, P]], base=0, channel_multiplier=0))
            pool.tensor_copy(rcnt, rcnt_i)
            pool.tensor_copy(tokf[:, :], toki[:, :])
            link(pool.tensor_copy(iotaf[:, :], iotai))
            pool.tensor_copy(iotap[:, :], iotaf[:, :]).then_inc(s_const, 1)

            def rms(i, count):
                r = ROWS[i]
                pool.wait_ge(s_sq, count + i + 1)
                link(pool.tensor_scalar(ss[0:r, i:i + 1], ss[0:r, i:i + 1], 1.0 / DM, EPS, ALU.mult, ALU.add))
                pool.tensor_tensor(rstd[0:r, i:i + 1], ss[0:r, i:i + 1], neg_half[0:r, :], ALU.pow
                                   ).then_inc(s_rstd, 1)

            for i in range(NT):
                rms(i, 0)
            for g in range(H):
                if g == 0:
                    wait_drained(pool, "buf")
                else:
                    pool.wait_ge(s_pooled, g)
                src = uext[:, g, :]
                at = 0
                for k in range(g + 1):
                    w = 1 << k
                    dst = wsum[:, k % 2, :]
                    at += w
                    ins = pool.tensor_tensor(dst[:, at:EXT], src[:, at:EXT], src[:, at - w:EXT - w], ALU.add)
                    if k == g:
                        ins.then_inc(s_wsum, 1)
                    else:
                        link(ins)
                    src = dst
            for h in range(H):
                for j in range(NP_):
                    pool.wait_ge(s_exp, NP_ * h + j + 1)
                    blk = D[:, BLK[j]:BLK[j] + P]
                    ins = pool.tensor_tensor(blk, blk, tri[:, :], ALU.mult)
                    link(ins)
                    pool.tensor_copy(wcol[:, j, h:h + 1], D[:, BLK[j + 1] - 1:BLK[j + 1]]).then_inc(s_msk, 1)
            pool.wait_ge(s_exps, 1)
            pool.tensor_tensor(Ds, Ds, bd.unsqueeze(1).to_broadcast([NS, H, NS]), ALU.mult).then_inc(s_msks, 1)
            for n, (r, i0, i1) in enumerate(((P, 0, NP_), (NS, NP_, NT))):
                pool.wait_ge(s_var, n + 1)
                nh = neg_half[0:r, :].unsqueeze(2).to_broadcast([r, i1 - i0, H])
                pool.tensor_tensor(fac[0:r, 3, i0:i1, :], fac[0:r, 2, i0:i1, :], nh, ALU.pow).then_inc(s_pw, 1)
            wait_drained(pool, "haT", NT - 1)
            pool.wait_ge(s_stat, 16 * STORES)
            link(pool.memset(lower, 1.0))
            pool.affine_select(out=lower, in_=lower, compare_op=ALU.is_ge, fill=0.0, base=-1,
                               pattern=[[1, NG], [-1, NG]], channel_multiplier=0)
            link(pool.memset(table[:, NE:NEX + 3, :], 0.0))
            pool.memset(table[:, NE:NEX + 3, 0:NT], -1.0).then_inc(s_const, 1)
            for i in range(NT):
                rms(i, NT)

            for k in range(2):
                pool.wait_ge(s_xsd[k], 16 * (3 - k))
            after(pool, "x2T", NT - 1, 1)
            pool.memset(xg[0], 0.0)
            for k in (2, 3):
                pool.memset(slot[k][:, :], FAR)
            link(pool.memset(xg[1], 0.0))
            for b in range(2):
                pool.indirect_dma_start(ex_dram, bass.IndirectOffsetOnAxis(slot[2 + b][:, 1:2], 0), xg[b], None,
                                        bounds_check=T * K - 1, oob_is_err=False).then_inc(s_scatter[b], 16)
            for b in range(2):
                pool.wait_ge(s_scatter[b], 16)

            def wait_on_its_own():
                pool.sem_inc(s_carried, 1)

            def gather(base, n, k, b):
                pool.wait_ge(s_index, base + n)
                wait_on_its_own()
                pool.indirect_dma_start(xg[b], None, xs_dram,
                                        bass.IndirectOffsetOnAxis(slot[k][:, 0:1], 0),
                                        bounds_check=T - 1, oob_is_err=False).then_inc(s_gather[b], 16)

            pool.wait_ge(s_np, 1)
            passes = pool.value_load(np_i[0:1, 0:1], min_val=1, max_val=PASSES)
            with pool.Fori(0, passes, 1) as r:
                gather(r * NEX, 1, 0, 0)
                gather(r * NEX, 2, 1, 1)
                with pool.Fori(0, NE, 4) as n:
                    for j in range(4):
                        pool.wait_ge(s_pxt, r * (NE + 1) + n + (j + 1))
                        gather(r * NEX + n, j + 3, (j + 2) % 4, j % 2)
                        pool.wait_ge(s_out0, r * NE + n + (j + 1))
                        pool.wait_ge(s_out1, r * NE + n + (j + 1))
                        wait_on_its_own()
                        pool.indirect_dma_start(ex_dram, bass.IndirectOffsetOnAxis(slot[j][:, 1:2], 0),
                                                og[j % 2], None, bounds_check=T * K - 1,
                                                oob_is_err=False).then_inc(s_scatter[j % 2], 16)
                pool.wait_ge(s_pxt, (r + 1) * (NE + 1))
            for b in range(2):
                pool.wait_ge(s_scatter[b], passes * (NE // 2 * 16) + 16)
            pool.wait_ge(s_mm2, passes * NE)
            wait_on_its_own()
            for i in range(NT):
                for k in range(K):
                    if i:
                        pool.wait_ge(s_x2, K * (i - 1) + k + 1)
                    r = ROWS[i]
                    pool.indirect_dma_start(cg[k][0:r, :], None, ex_dram,
                                            bass.IndirectOffsetOnAxis(keyi[0:r, i, k:k + 1], 0),
                                            bounds_check=T * K - 1, oob_is_err=False).then_inc(s_cg[k], 16)
                if i:
                    rms(i - 1, 2 * NT)
            rms(NT - 1, 2 * NT)
            for i in range(NT):
                rms(i, 3 * NT)

        @block.scalar
        def _(act):
            def square(i, n):
                r = ROWS[i]
                act.activation(junk[0:r, :], x[0:r, i, :], ACT.Square, accum_out=ss[0:r, i:i + 1]).then_inc(s_sq, 1)
                act.wait_ge(s_sq, n)

            for i in range(NT + 1):
                if i < NT:
                    act.wait_ge(s_x[i], 16)
                    square(i, i + 1)
                if i >= 1:
                    b = full_bank(act, "x1T", i - 1, 1)
                    r = ROWS[i - 1]
                    drain("s", act.copy(xT[:, 4:8, tok(i - 1)], b[:, :].rearrange("p (c t) -> p c t", t=P)[:, :, 0:r]),
                          "x1T", i - 1, 1)
            act.wait_ge(s_abs, 1)
            act.activation(r_e, r_e, ACT.Exp, scale=-1.0).then_inc(act_step, 1)
            act.wait_ge(act_step, 1)
            act.activation(r_l, r_e, ACT.Ln, bias=1.0).then_inc(s_ln, 1)
            for j in range(H):
                for n in range(2):
                    b = full_bank(act, "q", j, n)
                    drain("s", act.mul(qT[:, j, TH * n:TH * n + TH], b[:, 0:TH], float(P) ** -0.5), "q", j, n)
            act.wait_ge(s_mrow, 1)
            act.activation(em_row, m_row, ACT.Exp, scale=-1.0)
            act.activation(srow[:, NS:2 * NS + NB], srow[:, NS:2 * NS + NB], ACT.Exp).then_inc(s_em, 1)
            for j in range(H):
                for n in range(2):
                    b = full_bank(act, "k", j, n)
                    drain("s", act.copy(kT[:, j, TH * n:TH * n + TH], b[:, 0:TH]), "k", j, n)
            act.wait_ge(s_small, 16 * 5)
            for j in range(H):
                for n in range(2):
                    b = full_bank(act, "mix", j, n)
                    drain("s", act.activation(mixT[:, H + j, TH * n:TH * n + TH], b[:, 0:TH], ACT.Copy,
                                              scale=pl_s[:, j:j + 1]), "mix", j, n)
            b = full_bank(act, "pp")
            drain("s", act.copy(ppo, b[0:R, :]), "pp")
            b = full_bank(act, "ps")
            drain("s", act.copy(pso, b[0:NS, :]), "ps")
            for h in range(H):
                for j in range(NP_):
                    act.wait_ge(s_dif, NP_ * h + j + 1)
                    blk = D[:, BLK[j]:BLK[j + 1]]
                    act.activation(blk, blk, ACT.Exp, scale=-1.0).then_inc(s_exp, 1)
                b = full_bank(act, "o", h)
                drain("s", act.activation(so[:, h, :], b[:, :], ACT.Tanh, scale=0.5), "o", h)
                for i in range(NP_):
                    b = full_bank(act, "num", h, i)
                    drain("s", act.copy(nb[:, i, h, :], b[:, 0:DE]), "num", h, i)
            wait_drained(act, "num", H - 1, NP_ - 1)
            for i in range(NP_):
                for h in range(H):
                    ins = act.activation(junk[:, 0:P], nb[:, i, h, 0:P], ACT.Square, accum_out=fac[:, 0, i, h:h + 1])
                    ins.then_inc(s_sqh, 1)
                    act.wait_ge(s_sqh, H * i + h + 1)
            act.wait_ge(s_difs, 1)
            act.activation(Ds, Ds, ACT.Exp, scale=-1.0).then_inc(s_exps, 1)
            for h in range(H):
                b = full_bank(act, "Cp", h)
                drain("s", act.copy(Cp[:, h, :], b[:, 0:DE]), "Cp", h)
            b = full_bank(act, "kns")
            drain("s", act.copy(kws, b[0:NS, :].rearrange("p (h d) -> p h d", d=P)), "kns")
            b = full_bank(act, "o", 4)
            drain("s", act.activation(so[0:NS, 4, :], b[0:NS, :], ACT.Tanh, scale=0.5), "o", 4)
            b = full_bank(act, "nT")
            drain("s", act.copy(numT, b[:, 0:H * NS].rearrange("p (h t) -> p h t", t=NS)), "nT")
            b = full_bank(act, "nTt")
            drain("s", act.copy(nb[0:NS, NP_, :, 0:P], b[0:NS, :].rearrange("p (h d) -> p h d", d=P)), "nTt")
            wait_drained(act, "nTt")
            for h in range(H):
                ins = act.activation(junk[0:NS, 0:P], nb[0:NS, NP_, h, 0:P], ACT.Square,
                                     accum_out=fac[0:NS, 0, NP_, h:h + 1])
                ins.then_inc(s_sqh, 1)
                act.wait_ge(s_sqh, H * NP_ + h + 1)
            b = full_bank(act, "nout")
            act.copy(nout[:, 0:P], b[0:NB * H, 0:P])
            drain("s", act.copy(nout[0:H, P:2 * P], b[0:H, P:2 * P]), "nout")

            def square2(i):
                act.wait_ge(s_x1, i + 1)
                square(i, NT + i + 1)

            def x2t(i):
                r = ROWS[i]
                b = full_bank(act, "x2T", i, 1)
                drain("s", act.copy(xT[:, 4:8, tok(i)], b[:, :].rearrange("p (c t) -> p c t", t=P)[:, :, 0:r]),
                      "x2T", i, 1)
                b = full_bank(act, "r", i)
                drain("s", act.activation(sc_[0:r, i, :], b[0:r, 0:NE], ACT.Tanh, scale=0.5), "r", i)
                b = full_bank(act, "sh", i)
                if i:
                    act.wait_ge(s_hsh, i)
                act.activation(hs[0:r, :], b[0:r, 0:FF], ACT.Silu).then_inc(s_silu_sh, 1)

            def sht(i):
                r = ROWS[i]
                b = full_bank(act, "shT", i)
                drain("s", act.copy(hT[:, :, 0:r], b[:, 0:2 * P].rearrange("p (c t) -> p c t", t=P)[:, :, 0:r]),
                      "shT", i)

            wait_drained(act, "haT", NT - 1)
            act.wait_ge(s_stat, 16 * STORES)
            square2(0)
            square2(1)
            x2t(0)
            square2(2)
            sht(0)
            x2t(1)
            square2(3)
            sht(1)
            x2t(2)
            square2(4)
            sht(2)
            x2t(3)
            for i in range(NT):
                b = full_bank(act, "pT", i)
                r = ROWS[i]
                drain("s", act.copy(pT[:, :, tok(i)], b[:, 0:2 * P].rearrange("p (c t) -> p c t", t=P)[:, :, 0:r]),
                      "pT", i)
            sht(3)
            x2t(4)

            def pj(i):
                r = ROWS[i]
                for n in range(2):
                    b = full_bank(act, "pj", i, n)
                    drain("s", act.copy(proj[0:r, i, 512 * n:512 * n + 512], b[0:r, :]), "pj", i, n)

            pj(0)
            pj(1)
            sht(4)
            for i in range(2, NT):
                pj(i)

            def xg_half(base, n, b):
                act.wait_ge(s_pxt, base + n)
                act.copy(xgT[b][:, 4:8, :], bank[1][:, :].rearrange("p (c t) -> p c t", t=P)).then_inc(s_xgT1, 1)

            act.wait_ge(s_np, 1)
            passes = act.value_load(np_i[0:1, 0:1], min_val=1, max_val=PASSES)
            with act.Fori(0, passes, 1) as r:
                xg_half(r * (NE + 1), 1, 0)
                with act.Fori(0, NE, 4) as n:
                    for j in range(4):
                        b = j % 2
                        blk = r * NE + n + (j + 1)
                        act.wait_ge(s_mm1, blk)
                        act.activation(hs, bank[2][:, 0:FF], ACT.Silu).then_inc(s_silu, 1)
                        xg_half(r * (NE + 1) + n, j + 2, 1 - b)
                        act.wait_ge(s_pht, blk)
                        act.copy(hT, bank[4][:, 0:2 * P].rearrange("p (c t) -> p c t", t=P)).then_inc(s_hT, 1)
                        act.wait_ge(s_mm2, blk)
                        act.wait_ge(s_scatter[b], r * (NE // 2 * 16) + n * 8 + (j // 2 + 1) * 16)
                        act.copy(og[b][:, 0:512], bank[5][:, :]).then_inc(s_out0, 1)
                act.wait_ge(s_xgT1, (r + 1) * (NE + 1))

            for i in range(NT):
                r = ROWS[i]
                act.wait_ge(s_x2, K * (i + 1))
                square(i, 2 * NT + i + 1)
                b = full_bank(act, "x3T", i, 1)
                drain("s", act.copy(xT[:, 4:8, tok(i)], b[:, :].rearrange("p (c t) -> p c t", t=P)[:, :, 0:r]),
                      "x3T", i, 1)
                for n in range(2):
                    b = full_bank(act, "gt", i, n)
                    if i >= 2 and n == 0:
                        act.wait_ge(s_x3, i - 1)
                    drain("s", act.activation(gsig[i % 2][0:r, 512 * n:512 * n + 512], b[0:r, :], ACT.Tanh,
                                              scale=0.5), "gt", i, n)
            for i in range(NT):
                act.wait_ge(s_x3, i + 1)
                square(i, 3 * NT + i + 1)

        @block.vector
        def _(dve):
            n_step = [0]

            def link(ins):
                n_step[0] += 1
                ins.then_inc(dve_step, 1)
                dve.wait_ge(dve_step, n_step[0])

            def swizzled(row, r):
                return row[0:r, :].rearrange("t (c p) -> t p c", p=P)

            def normalise(i, dst, g, count):
                r = ROWS[i]
                dve.wait_ge(s_rstd, count + i + 1)
                dve.scalar_tensor_tensor(out=swizzled(dst, r), in0=x[0:r, i, :].rearrange("t (p c) -> t p c", c=KT),
                                         scalar=rstd[0:r, i:i + 1],
                                         in1=g[0:r, :].rearrange("t (p c) -> t p c", c=KT),
                                         op0=ALU.mult, op1=ALU.mult).then_inc(s_xs, 1)

            def turned(key, i):
                b = full_bank(dve, key, i, 0)
                r = ROWS[i]
                drain("v", dve.tensor_copy(xT[:, 0:4, tok(i)],
                                           b[:, :].rearrange("p (c t) -> p c t", t=P)[:, :, 0:r]), key, i, 0)

            dve.wait_ge(s_ga, 16)
            for i in range(NT + 1):
                if i < NT:
                    if i >= 2:
                        after(dve, "x1T", i - 2, 1)
                    normalise(i, xs1[:, i % 2, :], g_a, 0)
                if i >= 1:
                    turned("x1T", i - 1)
            dve.wait_ge(s_small, 16 * 5)
            for n in range(2):
                b = full_bank(dve, "g", n)
                c = slice(TH * n, TH * n + TH)
                dve.tensor_scalar(r_i[:, c], b[0:H, 0:TH], gate_b[0:H, :], None, ALU.add)
                drain("v", dve.tensor_scalar(r_f[:, c], b[32:32 + H, 0:TH], gate_b[32:32 + H, :], None, ALU.add),
                      "g", n)
            wait_drained(dve, "g", 1)
            dve.scalar_tensor_tensor(out=r_e, in0=r_f, scalar=-1.0, in1=r_f, op0=ALU.mult, op1=ALU.max
                                     ).then_inc(s_abs, 1)
            dve.wait_ge(s_ln, 1)
            link(dve.scalar_tensor_tensor(out=r_l, in0=r_f, scalar=0.0, in1=r_l, op0=ALU.min, op1=ALU.subtract))
            dve.wait_ge(s_const, 3)
            link(dve.tensor_tensor_scan(r_e, keep, r_l, 0.0, ALU.mult, ALU.add))
            link(dve.tensor_tensor(a_row, r_i, r_e, ALU.subtract))
            link(dve.tensor_copy(r_f, a_row))
            link(dve.tensor_tensor(r_f[:, SEQ:T:DS], a_row[:, SEQ:T:DS], m0row, ALU.max))
            link(dve.tensor_tensor_scan(M_row, reset, r_f, 0.0, ALU.add, ALU.max))
            dve.tensor_tensor(m_row, r_e, M_row, ALU.add)
            dve.tensor_copy(srow[:, 0:NS], M_row[:, SEQ:T])
            m0b = m0row.unsqueeze(2).to_broadcast([H, NB, DS])
            dve.tensor_tensor(srow[:, NS:2 * NS].rearrange("p (b t) -> p b t", t=DS), m0b,
                              M_row[:, SEQ:T].rearrange("p (b t) -> p b t", t=DS), ALU.subtract)
            dve.tensor_tensor(srow[:, 2 * NS:2 * NS + NB], m0row, M_row[:, SEQ + DS - 1:T:DS], ALU.subtract
                              ).then_inc(s_mrow, 1)
            for g in range(H):
                dve.tensor_scalar(rcnt[:, g, :], rcnt[:, g, :], float(WINDOWS[g]), None, ALU.min)
            link(dve.memset(small[0:1, 30:31], 0.0))
            dve.reciprocal(rcnt, rcnt)
            dve.wait_ge(s_const, 3)
            for j in range(H):
                for n in range(2):
                    b = full_bank(dve, "u", j, n)
                    if n == 0:
                        ins = dve.tensor_copy(uext[:, j, R:R + TH], b[:, 0:TH])
                    else:
                        dve.tensor_copy(uext[:, j, R + TH:SEGP], b[:, 0:SEQ - TH])
                        dve.tensor_copy(us[:, j, :], b[:, SEQ - TH:TH])
                        ins = dve.tensor_copy(uext[:, j, SEGP:EXT].rearrange("p (b t) -> p b t", t=SEGS)[:, :, R:SEGS],
                                              b[:, SEQ - TH:TH].rearrange("p (b t) -> p b t", t=DS))
                    drain("v", ins, "u", j, n)
            b = full_bank(dve, "buf")
            for j in range(H):
                ins = dve.tensor_copy(uext[:, j, SEGP:EXT].rearrange("p (b t) -> p b t", t=SEGS)[:, :, 0:R],
                                      b[:, P * j:P * j + NB * R].rearrange("p (b t) -> p b t", t=R))
            drain("v", ins, "buf")
            link(dve.memset(small[0:1, 30:31], 0.0))

            def pooling(g):
                w = WINDOWS[g]
                win = wsum[:, g % 2, :]
                dst = pooled[:, g % 2, :]
                dve.wait_ge(s_wsum, g + 1)
                if g >= 2:
                    after(dve, "mix", g - 2, 1)
                dve.scalar_tensor_tensor(out=dst[:, 16:SEQ], in0=win[:, R + 16:SEGP], scalar=1.0 / w,
                                         in1=uext[:, g, R + 16:SEGP], op0=ALU.mult, op1=ALU.subtract)
                seg = slice(SEGP, EXT)
                dve.scalar_tensor_tensor(
                    out=dst[:, SEQ:T].rearrange("p (b t) -> p b t", t=DS),
                    in0=win[:, seg].rearrange("p (b t) -> p b t", t=SEGS)[:, :, R:SEGS], scalar=1.0 / w,
                    in1=uext[:, g, seg].rearrange("p (b t) -> p b t", t=SEGS)[:, :, R:SEGS],
                    op0=ALU.mult, op1=ALU.subtract)
                link(dve.tensor_tensor(dst[:, 0:16], win[:, R:R + 16], rcnt[:, g, :], ALU.mult))
                dve.tensor_tensor(dst[:, 0:16], dst[:, 0:16], uext[:, g, R:R + 16], ALU.subtract
                                  ).then_inc(s_pooled, 1)

            for i in range(NT):
                b = full_bank(dve, "v", i)
                r = ROWS[i]
                drain("v", dve.tensor_copy(v[0:r, i, :, 0:P], b[0:r, :].rearrange("p (h d) -> p h d", d=P)), "v", i)
                if i < 2:
                    pooling(i)
            b = full_bank(dve, "nat")
            nat = b[:, 0:2 * NT * H].rearrange("p (a i h) -> p a i h", i=NT, h=H)
            dve.tensor_copy(anat[:, :, 0:NP_, :], nat[:, :, 0:NP_, :])
            drain("v", dve.tensor_copy(anat[0:NS, :, NP_, :], nat[0:NS, :, NP_, :]), "nat")
            wait_drained(dve, "nat")
            pooling(2)
            pooling(3)
            for h in range(H):
                b = full_bank(dve, "Mb", h)
                if h:
                    dve.wait_ge(s_pt, NP_ * h)
                    dve.wait_ge(s_msk, NP_ * h)
                for j in range(NP_):
                    dve.tensor_scalar(D[:, BLK[j]:BLK[j + 1]], b[:, P * j:SEQ], anat[:, 0, j, h:h + 1], 0.0,
                                      ALU.subtract, ALU.max).then_inc(s_dif, 1)
                dve.wait_ge(s_dif, NP_ * h + NP_)
                drain("v", dve.memset(small[0:1, 30:31], 0.0), "Mb", h)
                if h:
                    after(dve, "num", h - 1, NP_ - 1)
                for j in range(NP_):
                    b = full_bank(dve, "S", h, j)
                    dve.wait_ge(s_msk, NP_ * h + j + 1)
                    drain("v", dve.tensor_tensor(PT[:, BLK[j]:BLK[j + 1]], b[:, 0:SEQ - P * j],
                                                 D[:, BLK[j]:BLK[j + 1]], ALU.mult), "S", h, j)
                wait_drained(dve, "S", h, NP_ - 1)
                dve.memset(small[0:1, 30:31], 0.0).then_inc(s_pt, NP_)
            def factors(n, r, i0, i1):
                f = [fac[0:r, k, i0:i1, :] for k in range(6)]
                nq = nb[0:r, i0:i1, :, P]
                link(dve.scalar_tensor_tensor(out=f[4], in0=nq, scalar=-1.0, in1=nq, op0=ALU.mult, op1=ALU.max))
                link(dve.tensor_tensor(f[4], f[4], anat[0:r, 1, i0:i1, :], ALU.max))
                link(dve.reciprocal(f[1], f[4]))
                dve.wait_ge(s_sqh, H * i1)
                link(dve.tensor_tensor(f[2], f[0], f[1], ALU.mult))
                link(dve.tensor_tensor(f[2], f[2], f[1], ALU.mult))
                dve.tensor_scalar(f[2], f[2], 1.0 / P, EPS, ALU.mult, ALU.add).then_inc(s_var, 1)
                dve.wait_ge(s_pw, n + 1)
                link(dve.scalar_tensor_tensor(out=f[5], in0=f[3], scalar=0.5, in1=f[1], op0=ALU.mult, op1=ALU.mult))

            for k in range(2):
                b = full_bank(dve, "Ms", k)
                ms = b[:, 0:2 * (2 * NS + NB)].rearrange("p (h n) -> p h n", h=2)
                hh2 = slice(2 * k, 2 * k + 2)
                dve.tensor_tensor(Ds[:, hh2, :], ms[0:NS, :, 0:NS],
                                  anat[0:NS, 0, NP_, hh2].unsqueeze(2).to_broadcast([NS, 2, NS]), ALU.subtract)
                dve.tensor_tensor(qw[:, hh2, :], ms[:, :, NS:2 * NS], qT[:, hh2, SEQ:T], ALU.mult)
                drain("v", dve.tensor_copy(fwb[:, hh2, :], ms[:, :, 2 * NS:2 * NS + NB]), "Ms", k)
            wait_drained(dve, "Ms", 1)
            dve.tensor_scalar(Ds, Ds, 0.0, None, ALU.max).then_inc(s_difs, 1)
            b = full_bank(dve, "Ss")
            dve.wait_ge(s_msks, 1)
            drain("v", dve.tensor_tensor(PTs, b[0:NS, 0:H * NS].rearrange("p (h t) -> p h t", t=NS), Ds, ALU.mult), "Ss")
            for h in range(H):
                b = full_bank(dve, "kn", h)
                if h >= 2:
                    after(dve, "Cp", h - 2)
                drain("v", dve.tensor_tensor(kw[:, h % 2], b[:, :].rearrange("p (j d) -> p j d", d=P),
                                             wcol[:, :, h:h + 1].to_broadcast([P, NP_, P]), ALU.mult), "kn", h)
            wait_drained(dve, "num", H - 1, NP_ - 1)
            factors(0, P, 0, NP_)
            b = full_bank(dve, "n0")
            dve.wait_ge(s_c0, 16 * (NB + 1))
            drain("v", dve.tensor_copy(C0[:, :, :, P], b[:, 0:NB * H].rearrange("p (b h) -> p b h", h=H)), "n0")
            b = full_bank(dve, "nqs")
            ins = dve.tensor_tensor(nq9, b[0:NS, 0:16 * H].rearrange("p (h c) -> p h c", c=16)[:, :, 0:NB + 1],
                                    bmask.unsqueeze(1).to_broadcast([NS, H, NB + 1]), ALU.mult)
            drain("v", ins, "nqs")
            wait_drained(dve, "nqs")
            link(dve.tensor_reduce(nb[0:NS, NP_, :, P], nq9, AX.X, ALU.add))
            for h in range(H):
                if h:
                    after(dve, "C", h - 1, 2)
                dve.tensor_tensor(Vb[0:NS], v[0:NS, NP_, h, :].unsqueeze(1).to_broadcast([NS, NB, DE]),
                                  Ds[:, h, DS - 1:NS:DS].unsqueeze(2).to_broadcast([NS, NB, DE]), ALU.mult
                                  ).then_inc(s_vb, 1)
                for c in range(3):
                    b = full_bank(dve, "C", h, c)
                    for k in range(3 * c, min(3 * c + 3, NB)):
                        ins = dve.scalar_tensor_tensor(out=C0[:, k, h, :], in0=C0[:, k, h, :],
                                                       scalar=fwb[:, h, k:k + 1],
                                                       in1=b[:, DE * (k - 3 * c):DE * (k - 3 * c + 1)],
                                                       op0=ALU.mult, op1=ALU.add)
                    drain("v", ins, "C", h, c)
            wait_drained(dve, "nTt")
            factors(1, NS, NP_, NT)

            def turn_ha(i):
                b = full_bank(dve, "haT", i)
                r = ROWS[i]
                drain("v", dve.tensor_tensor(
                    mixT[:, 0:H, tok(i)], b[:, :].rearrange("p (h t) -> p h t", t=P)[:, :, 0:r],
                    hn_g.unsqueeze(2).to_broadcast([P, H, r]), ALU.mult), "haT", i)

            for i in range(NT):
                r = ROWS[i]
                if i >= 2:
                    after(dve, "haT", i - 2)
                wait_drained(dve, "o", i)
                hb = ha[0:r, i % 2, :]
                link(dve.tensor_tensor(hb.rearrange("p (h d) -> p h d", d=P), nb[0:r, i, :, 0:P],
                                       fac[0:r, 5, i, :].unsqueeze(2).to_broadcast([r, H, P]), ALU.mult))
                dve.scalar_tensor_tensor(out=hb, in0=so[0:r, i, :], scalar=1.0, in1=hb, op0=ALU.add, op1=ALU.mult
                                         ).then_inc(s_ha, 1)
                if i:
                    turn_ha(i - 1)
            turn_ha(NT - 1)

            dve.wait_ge(s_gb, 16)
            dve.wait_ge(s_stat, 16 * STORES)

            def add_x(key, i):
                r = ROWS[i]
                for n in range(2):
                    b = full_bank(dve, key, i, n)
                    c = slice(512 * n, 512 * n + 512)
                    drain("v", dve.tensor_tensor(x[0:r, i, c], b[0:r, :], x[0:r, i, c], ALU.add), key, i, n)
                wait_drained(dve, key, i, 1)

            def x1(i):
                add_x("wo", i)
                dve.memset(small[0:1, 30:31], 0.0).then_inc(s_x1, 1)

            def norm2(i):
                if i >= 2:
                    after(dve, "x2T", i - 2, 1)
                    dve.wait_ge(s_xsd[i % 2], 16 * (i // 2))
                normalise(i, xs2[i % 2], g_b, NT)

            def x2t(i):
                turned("x2T", i)
                r = ROWS[i]
                dve.wait_ge(s_silu_sh, i + 1)
                b = full_bank(dve, "sh", i)
                if i:
                    after(dve, "shT", i - 1)
                drain("v", dve.tensor_tensor(hh[0:r, :], b[0:r, FF:2 * FF], hs[0:r, :], ALU.mult), "sh", i)
                wait_drained(dve, "sh", i)
                dve.memset(small[0:1, 30:31], 0.0).then_inc(s_hsh, 1)

            x1(0)
            norm2(0)
            x1(1)
            norm2(1)
            x2t(0)
            x1(2)
            norm2(2)
            add_x("y", 0)
            x2t(1)
            x1(3)
            norm2(3)
            add_x("y", 1)
            x2t(2)
            x1(4)
            norm2(4)
            add_x("y", 2)
            x2t(3)
            add_x("y", 3)
            x2t(4)

            wait_drained(dve, "r", NT - 1)
            dve.wait_ge(s_rt, 32)
            link(dve.memset(sc_[NS:P, NP_, :], 0.0))
            link(dve.tensor_scalar(sc_, sc_, 0.5, 0.5, ALU.mult, ALU.add))
            link(dve.tensor_tensor(bi_, sc_, rbias.unsqueeze(1).to_broadcast([P, NT, NE]), ALU.add))
            g4 = [gs_[:, k] for k in range(8)]

            def by_group(t):
                return t.rearrange("p i (g k) -> p (i g) k", k=NG)

            def flat(t):
                return t.rearrange("p i g -> p (i g)")

            def spread(t, k=NG):
                return flat(t).unsqueeze(2).to_broadcast([P, NT * NG, k])

            link(dve.tensor_reduce(flat(g4[0]), by_group(bi_), AX.X, ALU.max))
            link(dve.tensor_tensor(by_group(t1_), by_group(bi_), spread(g4[0]), ALU.is_equal))
            link(dve.tensor_reduce(flat(g4[1]), by_group(t1_), AX.X, ALU.add))
            link(dve.scalar_tensor_tensor(out=t2_.rearrange("p i e -> p (i e)"),
                                          in0=t1_.rearrange("p i e -> p (i e)"), scalar=NEG,
                                          in1=bi_.rearrange("p i e -> p (i e)"), op0=ALU.mult, op1=ALU.add))
            link(dve.tensor_reduce(flat(g4[2]), by_group(t2_), AX.X, ALU.max))
            link(dve.tensor_scalar(g4[1], g4[1], 1.5, NEG, ALU.is_lt, ALU.mult))
            link(dve.tensor_tensor(g4[1], g4[1], g4[0], ALU.add))
            link(dve.tensor_tensor(g4[2], g4[2], g4[1], ALU.max))
            link(dve.tensor_tensor(g4[3], g4[0], g4[2], ALU.add))
            dve.wait_ge(s_const, 4)
            for i in range(NT):
                s = g4[3][:, i, :]
                row_a = s.unsqueeze(2).to_broadcast([P, NG, NG])
                row_b = s.unsqueeze(1).to_broadcast([P, NG, NG])
                ta = t1_[:, i, :].rearrange("p (a b) -> p a b", b=NG)
                tb = t2_[:, i, :].rearrange("p (a b) -> p a b", b=NG)
                dve.tensor_tensor(ta, row_b, row_a, ALU.is_gt)
                dve.tensor_tensor(tb, row_b, row_a, ALU.is_equal)
            link(dve.memset(small[0:1, 30:31], 0.0))
            low5 = lower.rearrange("p a b -> p (a b)").unsqueeze(1).to_broadcast([P, NT, NE])
            link(dve.tensor_tensor(t2_, t2_, low5, ALU.mult))
            link(dve.tensor_tensor(t1_, t1_, t2_, ALU.add))
            link(dve.tensor_reduce(flat(g4[4]), by_group(t1_), AX.X, ALU.add))
            link(dve.tensor_scalar(g4[5], g4[4], 3.5, None, ALU.is_lt))
            link(dve.tensor_scalar(g4[6], g4[5], -1.0, -NEG, ALU.add, ALU.mult))
            link(dve.tensor_tensor(by_group(t1_), by_group(bi_), spread(g4[5]), ALU.mult))
            link(dve.tensor_tensor(by_group(t1_), by_group(t1_), spread(g4[6]), ALU.add))
            for i in range(NT):
                dve.max(top[:, i, :], t1_[:, i, :])
            link(dve.memset(small[0:1, 30:31], 0.0))
            for i in range(NT):
                dve.match_replace(out=t2_[:, i, :], in_to_replace=top[:, i, :], in_values=t1_[:, i, :],
                                  imm_value=2 * NEG)
            link(dve.memset(small[0:1, 30:31], 0.0))
            link(dve.tensor_tensor(sel_, t1_, t2_, ALU.not_equal))
            link(dve.tensor_tensor(gt_, sc_, sel_, ALU.mult))
            link(dve.tensor_reduce(g4[7][:, :, 0], gt_, AX.X, ALU.add))
            link(dve.reciprocal(g4[7][:, :, 1], g4[7][:, :, 0]))
            link(dve.memset(sel_[NS:P, NP_, :], 0.0))
            dve.memset(small[0:1, 30:31], 0.0).then_inc(s_sel0, 1)
            link(dve.tensor_tensor(gt_, gt_, g4[7][:, :, 1:2].to_broadcast([P, NT, NE]), ALU.mult))
            add_x("y", 4)
            tb4 = table[:, 0:NE, :].rearrange("p e (c i) -> p c i e", i=NT)
            dve.tensor_scalar(tb4[:, 3], gt_, ROUTED_SCALE, None, ALU.mult)
            dve.tensor_copy(tb4[:, 1], tokf[:, :].unsqueeze(2).to_broadcast([P, NT, NE]))
            b = full_bank(dve, "pos")
            pos = b[:, 0:NT * NE].rearrange("p (i e) -> p i e", e=NE)
            counts = b[:, NT * NE:(NT + 1) * NE]
            link(dve.tensor_tensor_scan(ebase[:, :], onesf[:, 0:NE], counts, 0.0, ALU.mult, ALU.add))
            link(dve.scalar_tensor_tensor(out=ebase[:, :], in0=ebase[:, :], scalar=-float(FAR), in1=counts,
                                          op0=ALU.add, op1=ALU.subtract))
            dve.tensor_tensor(t2_, pos, ebase[:, :].unsqueeze(1).to_broadcast([P, NT, NE]), ALU.add)
            dve.tensor_scalar(t1_, pos, 1.0, None, ALU.add)
            drain("v", dve.tensor_reduce(np_f[0:1, 0:1], b[0:1, NT * NE:(NT + 1) * NE], AX.X, ALU.max), "pos")
            wait_drained(dve, "pos")
            dve.tensor_copy(tb4[:, 2], t2_)
            link(dve.tensor_tensor(t1_, t1_, sel_, ALU.mult))
            link(dve.tensor_scalar(tb4[:, 0], t1_, -1.0, None, ALU.add))
            link(dve.tensor_scalar(np_f[0:1, 1:2], np_f[0:1, 0:1], P + 0.5, 1.0, ALU.is_gt, ALU.add))
            for k in range(2, PASSES):
                link(dve.tensor_scalar(np_f[0:1, 2:3], np_f[0:1, 0:1], k * P + 0.5, None, ALU.is_gt))
                link(dve.tensor_tensor(np_f[0:1, 1:2], np_f[0:1, 1:2], np_f[0:1, 2:3], ALU.add))
            dve.tensor_copy(np_i[0:1, 0:1], np_f[0:1, 1:2]).then_inc(s_np, 1)
            link(dve.scalar_tensor_tensor(out=t2_.rearrange("p i e -> p (i e)"), in0=t2_.rearrange("p i e -> p (i e)"),
                                          scalar=float(FAR + 1), in1=sel_.rearrange("p i e -> p (i e)"),
                                          op0=ALU.add, op1=ALU.mult))
            for i in range(NT):
                dve.max(keys[:, i, :], t2_[:, i, :])
            link(dve.memset(small[0:1, 30:31], 0.0))
            link(dve.tensor_scalar(keyi[:, :, :], keys, -1.0, None, ALU.add))

            def one_hot(base, n, b, e):
                dve.tensor_copy(cols[b], table[:, bass.ds(e, 1), :].rearrange("p a c -> p (a c)")
                                ).then_inc(s_cols, 1)
                dve.wait_ge(s_cols, base + n)
                for i in range(NT):
                    ins = dve.tensor_scalar(onehot[b][:, i, :], iotap[:, :], cols[b][:, i:i + 1], None, ALU.is_equal)
                ins.then_inc(s_onehot, 1)

            def index(base, n, k):
                dve.wait_ge(s_psel, base + n)
                dve.tensor_copy(gate[k][:, :], bank[7][:, 2:3])
                dve.tensor_scalar(slot[k][:, :], bank[7][:, 0:2], float(FAR), None, ALU.add).then_inc(s_index, 1)

            def xg_half(base, n, b):
                dve.wait_ge(s_pxt, base + n)
                dve.tensor_copy(xgT[b][:, 0:4, :], bank[0][:, :].rearrange("p (c t) -> p c t", t=P)
                                ).then_inc(s_xgT0, 1)

            dve.wait_ge(s_np, 1)
            for b in range(2):
                dve.wait_ge(s_scatter[b], 16)
            passes = dve.value_load(np_i[0:1, 0:1], min_val=1, max_val=PASSES)
            with dve.Fori(0, passes, 1) as r:
                one_hot(r * NEX, 1, 0, 0)
                one_hot(r * NEX, 2, 1, 1)
                index(r * NEX, 1, 0)
                index(r * NEX, 2, 1)
                xg_half(r * (NE + 1), 1, 0)
                with dve.Fori(0, NE, 4) as n:
                    for j in range(4):
                        b = j % 2
                        blk = r * NE + n + (j + 1)
                        one_hot(r * NEX + n, j + 3, b, n + (j + 2))
                        dve.wait_ge(s_silu, blk)
                        dve.scalar_tensor_tensor(out=hh, in0=bank[2][:, FF:2 * FF], scalar=gate[j][:, 0:1], in1=hs,
                                                 op0=ALU.mult, op1=ALU.mult).then_inc(s_h, 1)
                        xg_half(r * (NE + 1) + n, j + 2, 1 - b)
                        index(r * NEX + n, j + 3, (j + 2) % 4)
                        dve.wait_ge(s_mm2, blk)
                        dve.wait_ge(s_scatter[b], r * (NE // 2 * 16) + n * 8 + (j // 2 + 1) * 16)
                        dve.tensor_copy(og[b][:, 512:DM], bank[6][:, :]).then_inc(s_out1, 1)
                dve.wait_ge(s_onehot, r * NEX + NEX)
                dve.tensor_scalar(iotap[:, :], iotap[:, :], float(P), None, ALU.add).then_inc(s_place, 1)
                dve.wait_ge(s_place, r + 1)
                for b in range(2):
                    dve.wait_ge(s_gather[b], (r + 1) * HG)
                dve.wait_ge(s_xgT0, (r + 1) * (NE + 1))

            def embed(i):
                r = ROWS[i]
                wait_drained(dve, "gt", i, 1)
                g = gsig[i % 2][0:r, :]
                link(dve.scalar_tensor_tensor(out=g, in0=g, scalar=1.0, in1=proj[0:r, i, :],
                                              op0=ALU.add, op1=ALU.mult))
                dve.scalar_tensor_tensor(out=x[0:r, i, :], in0=g, scalar=0.5, in1=x[0:r, i, :],
                                         op0=ALU.mult, op1=ALU.add).then_inc(s_x3, 1)

            dve.wait_ge(s_ga, 32)
            dve.wait_ge(s_gb, 32)
            for i in range(NT):
                r = ROWS[i]
                for k in range(K):
                    dve.wait_ge(s_cg[k], 16 * (i + 1))
                    dve.tensor_tensor(x[0:r, i, :], x[0:r, i, :], cg[k][0:r, :], ALU.add).then_inc(s_x2, 1)
                    dve.wait_ge(s_x2, K * i + k + 1)
                if i >= 2:
                    after(dve, "x3T", i - 2, 1)
                normalise(i, xs3[i % 2], g_a, 2 * NT)
                turned("x3T", i)
                if i:
                    embed(i - 1)
            embed(NT - 1)
            for i in range(NT):
                r = ROWS[i]
                dve.wait_ge(s_rstd, 3 * NT + i + 1)
                if i >= 2:
                    dve.wait_ge(s_yo[i % 2], 16 * (i // 2))
                dve.scalar_tensor_tensor(out=og[i % 2][0:r, :], in0=x[0:r, i, :], scalar=rstd[0:r, i:i + 1],
                                         in1=g_b[0:r, :], op0=ALU.mult, op1=ALU.mult).then_inc(s_y, 1)

        @block.tensor
        def _(pe):
            def turn(key, i, src):
                r = ROWS[i]
                for n in range(2):
                    b = free_bank(pe, key, i, n)
                    for c in range(4):
                        s = (4 * n + c) * P
                        ins = pe.transpose(b[:, P * c:P * c + r], src[0:r, s:s + P], ident[0:r, 0:r])
                    ins.then_inc(filled, 1)

            def reduce_over(b, lhs, rhs, nk):
                for c in range(nk):
                    ins = pe.matmul(b, lhs(c), rhs(c), start=(c == 0), stop=(c == nk - 1))
                return ins

            pe.wait_ge(s_const, 2)
            for i in range(NT):
                pe.wait_ge(s_xs, i + 1)
                turn("x1T", i, xs1[:, i % 2, :])
            wait_drained(pe, "x1T", NT - 1, 0)
            wait_drained(pe, "x1T", NT - 1, 1)
            pe.wait_ge(s_wg, 32)
            for n in range(2):
                b = free_bank(pe, "g", n)
                reduce_over(b[0:36, 0:TH], lambda c: wg[:, c, :], lambda c: xT[:, c, TH * n:TH * n + TH], KT
                            ).then_inc(filled, 1)
            for name in ("q", "k", "u"):
                chunk_in(pe, name)
                w = chunk(name).rearrange("p (c n) -> p c n", n=512)
                for j in range(H):
                    for n in range(2):
                        b = free_bank(pe, name, j, n)
                        reduce_over(b[:, 0:TH], lambda c: w[:, c, P * j:P * j + P],
                                    lambda c: xT[:, c, TH * n:TH * n + TH], KT).then_inc(filled, 1)
            pe.wait_ge(s_state, 32)
            b = free_bank(pe, "buf")
            for j in range(H):
                ins = pe.transpose(b[:, P * j:P * j + NB * R], bufnat[:, P * j:P * j + P], ident[0:NB * R, 0:NB * R])
            ins.then_inc(filled, 1)

            def natural(key, i):
                b = free_bank(pe, key, i)
                w = chunk(key).rearrange("p (c n) -> p c n", n=512)
                reduce_over(b[0:ROWS[i], :], lambda c: xT[:, c, tok(i)], lambda c: w[:, c, :], KT
                            ).then_inc(filled, 1)

            chunk_in(pe, "v")
            for i in range(NT):
                natural("v", i)
            pe.wait_ge(s_em, 1)
            b = free_bank(pe, "nat")
            for a, row in enumerate((a_row, em_row)):
                for i in range(NT):
                    n0 = (a * NT + i) * H
                    ins = pe.transpose(b[0:ROWS[i], n0:n0 + H], row[:, tok(i)], ident[0:H, 0:H])
            ins.then_inc(filled, 1)
            for j in range(H):
                pe.wait_ge(s_pooled, j + 1)
                for n in range(2):
                    b = free_bank(pe, "mix", j, n)
                    pe.matmul(b[:, 0:TH], wp[:, j, :], pooled[:, j % 2, TH * n:TH * n + TH], start=True, stop=True
                              ).then_inc(filled, 1)
            b = free_bank(pe, "pp")
            for j in range(H):
                ins = pe.transpose(b[0:R, P * j:P * j + P], uext[:, j, SEQ:SEGP], ident[:, :])
            ins.then_inc(filled, 1)
            b = free_bank(pe, "ps")
            for j in range(H):
                ins = pe.transpose(b[0:NS, P * j:P * j + P],
                                   us[:, j, :], ident[:, :])
            ins.then_inc(filled, 1)
            chunk_in(pe, "o")
            wait_drained(pe, "k", H - 1, 1)
            for h in range(H):
                b = free_bank(pe, "Mb", h)
                pe.matmul(b[:, :], sel4[:, h, :], M_row[:, 0:SEQ], start=True, stop=True).then_inc(filled, 1)
                for j in range(NP_):
                    b = free_bank(pe, "S", h, j)
                    pe.matmul(b[:, 0:SEQ - P * j], kT[:, h, P * j:P * j + P], qT[:, h, P * j:SEQ], start=True,
                              stop=True).then_inc(filled, 1)
                natural("o", h)
                wait_drained(pe, "S", h, NP_ - 1)
                for i in range(NP_):
                    b = free_bank(pe, "num", h, i)
                    for j in range(i + 1):
                        at = BLK[j] + P * (i - j)
                        ins = pe.matmul(b[:, 0:DE], PT[:, at:at + P], v[:, j, h, :], start=(j == 0), stop=(j == i))
                    ins.then_inc(filled, 1)
            W = 2 * NS + NB
            for k in range(2):
                b = free_bank(pe, "Ms", k)
                for h in (2 * k, 2 * k + 1):
                    ins = pe.matmul(b[:, W * (h % 2):W * (h % 2 + 1)], sel4[:, h, :], srow, start=True, stop=True)
                ins.then_inc(filled, 1)
            b = free_bank(pe, "Ss")
            for h in range(H):
                ins = pe.matmul(b[0:NS, NS * h:NS * h + NS], kT[:, h, SEQ:T], qT[:, h, SEQ:T], start=True, stop=True)
            ins.then_inc(filled, 1)
            for h in range(H):
                b = free_bank(pe, "kn", h)
                for j in range(NP_):
                    ins = pe.transpose(b[:, P * j:P * j + P], kT[:, h, P * j:P * j + P], ident[:, :])
                ins.then_inc(filled, 1)
                wait_drained(pe, "kn", h)
                b = free_bank(pe, "Cp", h)
                reduce_over(b[:, 0:DE], lambda c: kw[:, h % 2, c, :], lambda c: v[:, c, h, :], NP_).then_inc(filled, 1)
            b = free_bank(pe, "kns")
            for h in range(H):
                ins = pe.transpose(b[0:NS, P * h:P * h + P], kT[:, h, SEQ:T], ident[:, :])
            ins.then_inc(filled, 1)
            pe.wait_ge(s_c0, 16 * (NB + 1))
            b = free_bank(pe, "n0")
            pe.transpose(b[:, 0:NB * H], n0nat, ident[0:NB * H, 0:NB * H]).then_inc(filled, 1)
            natural("o", 4)
            wait_drained(pe, "Ss")
            wait_drained(pe, "n0")
            b = free_bank(pe, "nT")
            for h in range(H):
                pe.matmul(b[:, NS * h:NS * h + NS], v[0:NS, NP_, h, 0:P], PTs[:, h, :], start=True, stop=False,
                          skip_group_check=True)
                for k in range(NB):
                    c = NS * h + DS * k
                    ins = pe.matmul(b[:, c:c + DS], C0[:, k, h, 0:P], qw[:, h, DS * k:DS * k + DS], start=False,
                                    stop=(k == NB - 1), skip_group_check=True)
            ins.then_inc(filled, 1)
            b = free_bank(pe, "nqs")
            for h in range(H):
                pe.matmul(b[0:NS, 16 * h:16 * h + NB], qw[:, h, :], C0[:, :, h, P], start=True, stop=True)
                ins = pe.matmul(b[0:NS, 16 * h + NB:16 * h + NB + 1], PTs[:, h, :], onesf[0:NS, 0:1], start=True,
                                stop=True)
            ins.then_inc(filled, 1)
            wait_drained(pe, "nT")
            b = free_bank(pe, "nTt")
            for h in range(H):
                ins = pe.transpose(b[0:NS, P * h:P * h + P], numT[:, h, :], ident[:, :])
            ins.then_inc(filled, 1)
            wait_drained(pe, "kns")
            for h in range(H):
                pe.wait_ge(s_vb, h + 1)
                for c in range(3):
                    nb_ = min(3, NB - 3 * c)
                    b = free_bank(pe, "C", h, c)
                    pe.matmul(b[:, 0:nb_ * DE], kws[:, h, :], Vb[0:NS, 3 * c:3 * c + nb_, :], start=True, stop=True
                              ).then_inc(filled, 1)
            for i in range(NT):
                pe.wait_ge(s_ha, i + 1)
                b = free_bank(pe, "haT", i)
                r = ROWS[i]
                for h in range(H):
                    ins = pe.transpose(b[:, P * h:P * h + r], ha[0:r, i % 2, P * h:P * h + P], ident[0:r, 0:r])
                ins.then_inc(filled, 1)
            wait_drained(pe, "Cp", H - 1)
            b = free_bank(pe, "nout")
            pe.transpose(b[0:NB * H, 0:P], C0[:, :, :, P].rearrange("p b h -> p (b h)"), ident[:, :])
            pe.transpose(b[0:H, P:2 * P], Cp[:, :, P], ident[:, :]).then_inc(filled, 1)

            def wo(i):
                for n in range(2):
                    chunk_in(pe, f"wo{n}")
                    b = free_bank(pe, "wo", i, n)
                    w = chunk(f"wo{n}").rearrange("p (c n) -> p c n", n=512)
                    reduce_over(b[0:ROWS[i], :], lambda c: mixT[:, c, tok(i)], lambda c: w[:, c, :], KT
                                ).then_inc(filled, 1)

            def norm2(i):
                r = ROWS[i]
                pe.wait_ge(s_xs, NT + i + 1)
                turn("x2T", i, xs2[i % 2])
                wait_drained(pe, "x2T", i, 0)
                wait_drained(pe, "x2T", i, 1)
                b = free_bank(pe, "r", i)
                reduce_over(b[0:r, 0:NE], lambda c: xT[:, c, tok(i)], lambda c: rw[:, c, :], KT).then_inc(filled, 1)
                b = free_bank(pe, "sh", i)
                reduce_over(b[0:r, :], lambda c: xT[:, c, tok(i)], lambda c: w13[1][:, :, c, :], KT
                            ).then_inc(filled, 1)

            def shared(i):
                r = ROWS[i]
                pe.wait_ge(s_hsh, i + 1)
                b = free_bank(pe, "shT", i)
                for c in range(2):
                    ins = pe.transpose(b[:, P * c:P * c + r], hh[0:r, P * c:P * c + P], ident[0:r, 0:r])
                ins.then_inc(filled, 1)
                wait_drained(pe, "shT", i)
                for n in range(2):
                    b = free_bank(pe, "y", i, n)
                    reduce_over(b[0:r, :], lambda c: hT[:, c, 0:r], lambda c: w2s[1][:, c, 512 * n:512 * n + 512], 2
                                ).then_inc(filled, 1)

            wait_drained(pe, "haT", NT - 1)
            wo(0)
            wo(1)
            pe.wait_ge(s_rt, 32)
            pe.wait_ge(s_sh, 48)
            norm2(0)
            wo(2)
            shared(0)
            norm2(1)
            wo(3)
            shared(1)
            norm2(2)
            wo(4)
            shared(2)
            norm2(3)
            pe.wait_ge(s_p, 16 * NT)
            for i in range(NT):
                r = ROWS[i]
                b = free_bank(pe, "pT", i)
                for c in range(2):
                    ins = pe.transpose(b[:, P * c:P * c + r], ptile[0:r, i, P * c:P * c + P], ident[0:r, 0:r])
                ins.then_inc(filled, 1)
            shared(3)
            norm2(4)

            def pj(i):
                r = ROWS[i]
                w = chunk("pj")[:, 0:2 * DM].rearrange("p (c n) -> p c n", n=DM)
                for n in range(2):
                    b = free_bank(pe, "pj", i, n)
                    reduce_over(b[0:r, :], lambda c: pT[:, c, tok(i)], lambda c: w[:, c, 512 * n:512 * n + 512], 2
                                ).then_inc(filled, 1)

            chunk_in(pe, "pj")
            wait_drained(pe, "pT", NT - 1)
            pj(0)
            pj(1)
            shared(4)
            for i in range(2, NT):
                pj(i)
            pe.wait_ge(s_sel0, 1)
            b = free_bank(pe, "pos")
            for i in range(NT + 1):
                for k in range(min(i + 1, NT)):
                    ins = pe.matmul(b[:, NE * i:NE * i + NE], before[:, :] if k == i else onesf[:, :], sel_[:, k, :],
                                    start=(k == 0), stop=(k == min(i, NT - 1)))
            ins.then_inc(filled, 1)

            def pick(base, n, b):
                pe.wait_ge(s_onehot, base + n)
                c = cols[b].rearrange("p (c i) -> p c i", i=NT)
                for i in range(NT):
                    ins = pe.matmul(bank[7][:, 0:3], onehot[b][:, i, :], c[:, 1:4, i], start=(i == 0),
                                    stop=(i == NT - 1))
                ins.then_inc(s_psel, 1)

            def turn_rows(gathers, b):
                pe.wait_ge(s_gather[b], gathers)
                for c in range(8):
                    ins = pe.transpose(bank[c // 4][:, P * (c % 4):P * (c % 4) + P], xg[b][:, P * c:P * c + P],
                                       ident[:, :])
                ins.then_inc(s_pxt, 1)

            wait_drained(pe, "pos")
            wait_drained(pe, "pj", NT - 1, 1)
            pe.wait_ge(s_np, 1)
            passes = pe.value_load(np_i[0:1, 0:1], min_val=1, max_val=PASSES)
            with pe.Fori(0, passes, 1) as r:
                pick(r * NEX, 1, 0)
                pe.wait_ge(s_index, r * NEX + 1)
                pick(r * NEX, 2, 1)
                turn_rows(r * HG + 16, 0)
                with pe.Fori(0, NE, 4) as n:
                    for j in range(4):
                        b = j % 2
                        blk = r * NE + n + (j + 1)
                        pe.wait_ge(s_w13[b], r * (NE // 2 * 32) + n * 16 + (j // 2 + 1) * 32)
                        pe.wait_ge(s_xgT0, r * (NE + 1) + n + (j + 1))
                        pe.wait_ge(s_xgT1, r * (NE + 1) + n + (j + 1))
                        for c in range(KT):
                            ins = pe.matmul(bank[2][:, :], xgT[b][:, c, :], w13[b][:, :, c, :], start=(c == 0),
                                            stop=(c == KT - 1))
                        ins.then_inc(s_mm1, 1)
                        turn_rows(r * HG + n * 8 + (16 if j < 1 else 32 if j < 3 else 48), 1 - b)
                        pe.wait_ge(s_h, blk)
                        for c in range(2):
                            ins = pe.transpose(bank[4][:, P * c:P * c + P], hh[:, P * c:P * c + P], ident[:, :])
                        ins.then_inc(s_pht, 1)
                        pe.wait_ge(s_index, r * NEX + n + (j + 2))
                        pick(r * NEX + n, j + 3, b)
                        pe.wait_ge(s_hT, blk)
                        pe.wait_ge(s_w2[b], r * (NE // 2 * 16) + n * 8 + (j // 2 + 1) * 16)
                        for half in range(2):
                            for c in range(2):
                                ins = pe.matmul(bank[5 + half][:, :], hT[:, c, :],
                                                w2s[b][:, c, 512 * half:512 * half + 512], start=(c == 0),
                                                stop=(c == 1))
                        ins.then_inc(s_mm2, 1)
            pe.wait_ge(s_out0, passes * NE)
            pe.wait_ge(s_out1, passes * NE)
            pe.wait_ge(s_xgT0, passes * (NE + 1))
            pe.wait_ge(s_xgT1, passes * (NE + 1))
            pe.wait_ge(s_index, passes * NEX)

            for i in range(NT):
                r = ROWS[i]
                pe.wait_ge(s_xs, 2 * NT + i + 1)
                turn("x3T", i, xs3[i % 2])
                wait_drained(pe, "x3T", i, 0)
                wait_drained(pe, "x3T", i, 1)
                for n in range(2):
                    chunk_in(pe, f"gt{n}")
                    b = free_bank(pe, "gt", i, n)
                    w = chunk(f"gt{n}").rearrange("p (c n) -> p c n", n=512)
                    reduce_over(b[0:r, :], lambda c: xT[:, c, tok(i)], lambda c: w[:, c, :], KT
                                ).then_inc(filled, 1)


_INS = ["x_prompt", "x_sample", "p_prompt", "p_sample", "state_C", "state_n", "state_m", "state_pool",
        "norm_mix_g", "w_in", "b_igate", "b_fgate", "head_norm_g", "w_pool", "pool_scale", "w_out",
        "norm_ffn_g", "router_w", "router_bias", "ex_w1", "ex_w3", "ex_w2", "sh_w1", "sh_w3", "sh_w2",
        "norm_ple_g", "w_ple_gate", "w_ple_proj", "final_norm_g"]
_OUTS = ["y_prompt", "y_sample", "C_prompt", "n_prompt", "m_prompt", "pool_prompt",
         "C_sample", "n_sample", "m_sample", "pool_sample"]


def kernel(**inputs):
    import numpy as _np
    import concourse.bacc as _bacc
    from concourse import mybir as _mybir
    from concourse.bass_utils import run_bass_kernel_spmd as _run

    nc = _bacc.Bacc("TRN2", target_bir_lowering=False, num_devices=1)
    arrays, args = {}, []
    for name in _INS:
        a = _np.ascontiguousarray(inputs[name])
        arrays[f"in_{name}"] = a
        args.append(nc.dram_tensor(f"in_{name}", a.shape, _mybir.dt.from_np(a.dtype), kind="ExternalInput").ap())
    depth, batch = inputs["p_prompt"].shape[:2]
    heads, dh = inputs["state_n"].shape[2:]
    rows, width = inputs["state_pool"].shape[2:]
    nb = inputs["x_sample"].shape[0]
    shapes = [inputs["x_prompt"].shape, inputs["x_sample"].shape]
    for b in (batch, nb):
        shapes += [(depth, b, heads, dh, dh), (depth, b, heads, dh), (depth, b, heads), (depth, b, rows, width)]
    for name, shape in zip(_OUTS, shapes):
        args.append(nc.dram_tensor(f"out_{name}", shape, _mybir.dt.float32, kind="ExternalOutput").ap())
    decoder_step(nc, *args)
    r = _run(nc, [arrays], core_ids=[0])
    return tuple(r.results[0][f"out_{name}"] for name in _OUTS)
```

```python
from contextlib import ExitStack

import concourse.bass as bass
from concourse import mybir

F32 = mybir.dt.float32
I32 = mybir.dt.int32
BF16 = mybir.dt.bfloat16
ALU = mybir.AluOpType
ACT = mybir.ActivationFunctionType
AX = mybir.AxisListType

P = 128
EPS = 1e-6
NEG = -1e30
FAR = 1 << 14
ROUTED_SCALE = 2.5
WINDOWS = (2, 4, 8, 16)


def psum_groups(NT, H, KH):
    g = []
    for i in range(NT):
        g += [(("x1T", i, 0), "v"), (("x1T", i, 1), "s")]
    g += [(("g", 0), "v"), (("g", 1), "v")]
    g += [(("q", j, n), "s") for j in range(H) for n in range(2)]
    g += [(("k", j, n), "s") for j in range(H) for n in range(2)]
    g += [(("u", j, n), "v") for j in range(H) for n in range(2)]
    g += [(("buf",), "v")]
    g += [(("v", i), "v") for i in range(NT)]
    g += [(("nat",), "v")]
    g += [(("mix", j, n), "s") for j in range(H) for n in range(2)]
    g += [(("pp",), "s"), (("ps",), "s")]
    for h in range(H):
        g += [(("Mb", h), "v")] + [(("S", h, j), "v") for j in range(4)]
        g += [(("o", h), "s")]
        g += [(("num", h, i), "s") for i in range(4)]
    g += [(("Ms", 0), "v"), (("Ms", 1), "v"), (("Ss",), "v")]
    for h in range(H):
        g += [(("kn", h), "v"), (("Cp", h), "s")]
    g += [(("kns",), "s"), (("n0",), "v"), (("o", 4), "s"), (("nT",), "s"), (("nqs",), "v"), (("nTt",), "s")]
    g += [(("C", h, c), "v") for h in range(H) for c in range(3)]
    g += [(("haT", i), "v") for i in range(NT)]
    g += [(("nout",), "s")]

    def wo(i):
        return [(("wo", i, 0), "v"), (("wo", i, 1), "v")]

    def norm2(i):
        return [(("x2T", i, 0), "v"), (("x2T", i, 1), "s"), (("r", i), "s"), (("sh", i), "v")]

    def shared(i):
        return [(("shT", i), "s"), (("y", i, 0), "v"), (("y", i, 1), "v")]

    g += wo(0) + wo(1) + norm2(0) + wo(2) + shared(0) + norm2(1) + wo(3) + shared(1) + norm2(2)
    g += wo(4) + shared(2) + norm2(3)
    g += [(("pT", i), "s") for i in range(NT)]
    g += shared(3) + norm2(4)
    g += [(("pj", i, n), "s") for i in range(2) for n in range(2)]
    g += shared(4)
    g += [(("pj", i, n), "s") for i in range(2, NT) for n in range(2)]
    g += [(("pos",), "v")]
    for i in range(NT + 1):
        if i < NT:
            g += [(("x3T", i, 0), "v"), (("x3T", i, 1), "s")]
        if i:
            g += [(("gt", i - 1, 0), "s"), (("gt", i - 1, 1), "s")]
    return g


def decoder_step(nc, x_prompt, x_sample, p_prompt, p_sample, state_C, state_n, state_m, state_pool,
                 norm_mix_g, w_in, b_igate, b_fgate, head_norm_g, w_pool, pool_scale, w_out,
                 norm_ffn_g, router_w, router_bias, ex_w1, ex_w3, ex_w2, sh_w1, sh_w3, sh_w2,
                 norm_ple_g, w_ple_gate, w_ple_proj, final_norm_g,
                 y_prompt, y_sample, C_prompt, n_prompt, m_prompt, pool_prompt,
                 C_sample, n_sample, m_sample, pool_sample):
    _, SEQ, DM = x_prompt.shape
    NB, DS, _ = x_sample.shape
    H = state_C.shape[2]
    NE = ex_w1.shape[1]
    FF = ex_w1.shape[3]
    PLE = p_prompt.shape[3]
    R = state_pool.shape[2]
    NP_ = SEQ // P
    NT = NP_ + 1
    NS = NB * DS
    T = SEQ + NS
    TH = T // 2
    KT = DM // P
    MW = H * P
    DE = P + 1
    ROWS = [P] * NP_ + [NS]
    SEGP = R + SEQ
    SEGS = R + DS
    EXT = SEGP + NB * SEGS
    NG = 8
    K = 8
    PASSES = -(-T // P)
    NEX = NE + 2
    TE = NE + 6
    NOH = NE + 3
    assert (SEQ, NS, DM, H, NE, FF, PLE, R) == (512, 64, 1024, 4, 64, 256, 256, 15)
    STORES = 1 + 1 + NB + 2 + 1 + NB + 2
    BLK = [0]
    for j in range(NP_):
        BLK.append(BLK[-1] + SEQ - P * j)

    ctx = ExitStack()
    with ctx:
        def sb(name, shape, dt=F32):
            return ctx.enter_context(nc.sbuf_tensor(name, shape, dt))

        def sem(name):
            return ctx.enter_context(nc.semaphore(name))

        def tok(i):
            return slice(P * i, P * i + ROWS[i])

        xs_dram = nc.dram_tensor("xs_dram", [T, DM], F32).ap()
        y_dram = nc.dram_tensor("y_dram", [T + P, DM], F32).ap()

        x = sb("x", [P, NT, DM])
        xT = sb("xT", [P, KT, T])
        mixpj = sb("mixpj", [P, NT * DM])
        mixT = mixpj[:, 0:KT * T].rearrange("p (c t) -> p c t", t=T)
        proj = mixpj[:, :].rearrange("p (i n) -> p i n", n=DM)
        ring = sb("ring", [P, 2, KT * 512])
        g_a = sb("g_a", [P, DM])
        g_b = sb("g_b", [P, DM])
        ident = sb("ident", [P, P])
        tri = sb("tri", [P, P])
        before = sb("before", [P, P])
        onesf = sb("onesf", [P, P])
        iotaf = sb("iotaf", [P, P])
        iotap = sb("iotap", [P, P])
        small = sb("small", [P, 32])
        eps_c, neg_half = small[:, 0:1], small[:, 1:2]
        gate_b = small[:, 2:3]
        hn_g = small[:, 4:8]
        pl_s = small[:, 8:12]
        ss = sb("ss", [P, NT])
        rstd = sb("rstd", [P, NT])
        ssf = sb("ssf", [P, NT])
        rstdf = sb("rstdf", [P, NT])
        junk = sb("junk", [P, DM])

        ARENA = 25503
        arena = sb("arena", [P, ARENA])
        used = {"mixer": 0, "experts": 0}

        def carve(phase, n, at=None):
            if at is None:
                at = used[phase]
                used[phase] += n
                assert used[phase] <= ARENA
            return arena[:, at:at + n], at

        def mx(n):
            return carve("mixer", n)[0]

        def ex(n):
            return carve("experts", n)[0]

        def over(at, n):
            return carve("mixer", n, at)[0]

        qT_raw, q_at = carve("mixer", H * T)
        qT = qT_raw.rearrange("p (h t) -> p h t", t=T)
        kT = mx(H * T).rearrange("p (h t) -> p h t", t=T)
        pool_raw, pool_at = carve("mixer", H * EXT + 2 * EXT + 2 * T)
        uext = pool_raw[:, 0:H * EXT].rearrange("p (g t) -> p g t", t=EXT)
        wsum = pool_raw[:, H * EXT:(H + 2) * EXT].rearrange("p (b t) -> p b t", t=EXT)
        pooled = pool_raw[:, (H + 2) * EXT:].rearrange("p (b t) -> p b t", t=T)
        C0 = carve("mixer", NB * H * DE, pool_at)[0].rearrange("p (b h e) -> p b h e", h=H, e=DE)
        c_at = pool_at + NB * H * DE
        D, d_at = carve("mixer", BLK[-1])
        PT, pt_at = carve("mixer", BLK[-1])
        wg = over(pt_at, KT * 36).rearrange("p (c n) -> p c n", n=36)
        bufnat = over(pt_at + 288, MW)[0:NB * R, :]
        iotai = over(pt_at + 800, P).bitcast(I32)
        us = over(pt_at + 992, H * NS).rearrange("p (h t) -> p h t", t=NS)
        Vb = carve("mixer", NB * DE, pt_at)[0].rearrange("p (b e) -> p b e", e=DE)
        v = mx(NT * H * DE).rearrange("p (i h e) -> p i h e", h=H, e=DE)
        so_raw, so_at = carve("mixer", NT * MW)
        so = so_raw.rearrange("p (i n) -> p i n", n=MW)
        xs1 = carve("mixer", 2 * DM, so_at)[0].rearrange("p (b n) -> p b n", n=DM)
        nb_raw, nb_at = carve("mixer", NT * H * DE)
        nb = nb_raw.rearrange("p (i h e) -> p i h e", h=H, e=DE)
        rows4 = [carve("mixer", T, nb_at + k * T)[0][0:H, :] for k in range(4)]
        r_i, r_f, r_e, r_l = rows4
        a_row, M_row, m_row = (mx(T)[0:H, :] for _ in range(3))
        keep = over(d_at, T)[0:H, :]
        reset = over(d_at + T, T)[0:H, :]
        srow = mx(NS + NS + NB)[0:H, :]
        m0row = mx(NB)[0:H, :]
        em_row = mx(T)[0:H, :]
        anat = mx(2 * NT * H).rearrange("p (a i h) -> p a i h", i=NT, h=H)
        wcol = mx(NP_ * H).rearrange("p (j h) -> p j h", h=H)
        fwb = mx(H * NB).rearrange("p (h b) -> p h b", b=NB)
        sel4 = mx(H * P).rearrange("p (h n) -> p h n", n=P)[0:H]
        bd = mx(NS)[0:NS, :]
        bmask = mx(NB + 1)[0:NS, :]
        rcnt = mx(H * 16).rearrange("p (g n) -> p g n", n=16)
        rcnt_i = mx(H * 16).bitcast(I32).rearrange("p (g n) -> p g n", n=16)
        kw = over(d_at, 2 * MW).rearrange("p (b j d) -> p b j d", j=NP_, d=P)
        kws = over(c_at, MW).rearrange("p (h d) -> p h d", d=P)[0:NS]
        wp_raw, wp_at = carve("mixer", H * P)
        wp = wp_raw.rearrange("p (g d) -> p g d", d=P)
        Ds = over(wp_at, H * NS).rearrange("p (h t) -> p h t", t=NS)[0:NS]
        PTs = over(wp_at + H * NS, H * NS).rearrange("p (h t) -> p h t", t=NS)[0:NS]
        qw = mx(H * NS).rearrange("p (h t) -> p h t", t=NS)
        numT = over(c_at + MW, H * NS).rearrange("p (h t) -> p h t", t=NS)
        nq9 = mx(H * (NB + 1)).rearrange("p (h c) -> p h c", c=NB + 1)[0:NS]
        Cp = over(q_at + 2 * MW, H * DE).rearrange("p (h e) -> p h e", e=DE)
        n0nat = over(c_at + MW + H * NS, P)[0:NB * H, :]
        nout = over(c_at + MW + H * NS + P, 2 * P)[0:NB * H, :]
        ppo = mx(MW)[0:R, :]
        pso = mx(MW)[0:NS, :]
        fac = mx(6 * NT * H).rearrange("p (k i h) -> p k i h", i=NT, h=H)
        ha = over(q_at, 2 * MW).rearrange("p (b n) -> p b n", n=MW)

        w13, w2s = [], []
        for _ in range(2):
            w13.append(ex(2 * KT * FF).rearrange("p (w c f) -> p w c f", w=2, f=FF))
            w2s.append(ex(2 * DM).rearrange("p (c n) -> p c n", n=DM))
        xg = [ex(DM) for _ in range(2)]
        xgT = [ex(DM).rearrange("p (c t) -> p c t", t=P) for _ in range(2)]
        og_at = used["experts"]
        og = [ex(DM) for _ in range(2)]
        onehot = [ex(NT * P // 2).bitcast(BF16).rearrange("p (i t) -> p i t", t=P) for _ in range(2)]
        ex(KT * NE + NT * PLE + 2 * T - 2 * DM - NT * P)
        hs = ex(FF)
        hh = ex(FF)
        hT = ex(2 * P).rearrange("p (c t) -> p c t", t=P)
        NC = 4 * NT
        table = ex((TE) * NC).rearrange("p (e c) -> p e c", c=NC)
        tplace = table[:, :, 0:NT]
        tpick = table[:, :, NT:NC].bitcast(BF16).rearrange("p e (i c) -> p e i c", c=6)
        cols = [ex(NC) for _ in range(2)]
        sc_, bi_, t1_, t2_, sel_, gt_ = (ex(NT * NE).rearrange("p (i e) -> p i e", e=NE) for _ in range(6))
        gs_ = ex(8 * NT * NG).rearrange("p (k i g) -> p k i g", i=NT, g=NG)
        rbias = ex(NE)
        rw = arena[:, og_at:og_at + KT * NE].rearrange("p (c e) -> p c e", e=NE)
        p_at = og_at + KT * NE
        ptile = arena[:, p_at:p_at + NT * PLE].rearrange("p (i n) -> p i n", n=PLE)
        pT = arena[:, p_at + NT * PLE:p_at + NT * PLE + 2 * T].rearrange("p (c t) -> p c t", t=T)
        lower = ex(NG * NG).rearrange("p (a b) -> p a b", b=NG)
        top = ex(NT * K).rearrange("p (i k) -> p i k", k=K)
        place5 = [c[:, 0:NT] for c in cols]
        pick6 = [c[:, NT:NC].bitcast(BF16).rearrange("p (i c) -> p i c", i=NT) for c in cols]
        xs2 = xg
        xs3 = [a.rearrange("p c t -> p (c t)") for a in xgT]
        gsig = [arena[:, k * DM:(k + 1) * DM] for k in range(2)]
        partf = sb("partf", [P, NT])
        tilef = sb("tilef", [P, NT])
        toki = sb("toki", [P, 2 * NT], I32)
        binf = sb("binf", [P, 1])
        token = [sb(f"token{k}", [P, 1]) for k in range(2)]
        slot = [sb(f"slot{k}", [P, 1], I32) for k in range(4)]
        outrow = [sb(f"outrow{k}", [P, 1], I32) for k in range(2)]
        gate = [sb(f"gate{k}", [P, 1]) for k in range(4)]
        np_f = sb("np_f", [1, 4])
        np_i = sb("np_i", [1, 2], I32)

        bank = [ctx.enter_context(nc.psum_tensor(f"bank{k}", [P, 512], F32)) for k in range(8)]

        s_x = [sem(f"s_xin{i}") for i in range(NT)]
        s_small = sem("s_small")
        s_ga, s_gb = sem("s_ga"), sem("s_gb")
        s_ring = [sem("s_ring0"), sem("s_ring1")]
        s_wg = sem("s_wg")
        s_state = sem("s_state")
        s_c0 = sem("s_c0")
        s_const = sem("s_const")
        filled = sem("filled")
        drained = {"v": sem("drained_v"), "s": sem("drained_s")}
        s_sq = sem("s_sq")
        s_rstd = sem("s_rstd")
        s_sqf, s_rstdf = sem("s_sqf"), sem("s_rstdf")
        s_xs = sem("s_xs")
        s_abs, s_ln, s_mrow, s_em = sem("s_abs"), sem("s_ln"), sem("s_mrow"), sem("s_em")
        s_wsum, s_pooled = sem("s_wsum"), sem("s_pooled")
        s_dif, s_exp, s_msk, s_pt = sem("s_dif"), sem("s_exp"), sem("s_msk"), sem("s_pt")
        s_difs, s_exps, s_msks, s_vb, s_place = (sem(n) for n in ("s_difs", "s_exps", "s_msks", "s_vb", "s_place"))
        s_sqh, s_var, s_pw, s_ha = sem("s_sqh"), sem("s_var"), sem("s_pw"), sem("s_ha")
        s_stat = sem("s_stat")
        s_sh, s_p, s_rt = sem("s_sh"), sem("s_p"), sem("s_rt")
        s_x1 = sem("s_x1")
        s_silu_sh, s_hsh = sem("s_silu_sh"), sem("s_hsh")
        s_xsd = [sem("s_xsd0"), sem("s_xsd1")]
        s_sel0 = sem("s_sel0")
        s_np = sem("s_np")
        s_carried = sem("s_carried")
        s_w13 = [sem("s_w13a"), sem("s_w13b")]
        s_w2 = [sem("s_w2a"), sem("s_w2b")]
        s_gather = [sem("s_gather0"), sem("s_gather1")]
        s_scatter = [sem("s_scatter0"), sem("s_scatter1")]
        (s_cols, s_onehot, s_index, s_h, s_xgT0, s_out1, s_silu, s_xgT1, s_hT, s_out0,
         s_psel, s_pxt, s_mm1, s_pht, s_mm2) = (sem(n) for n in (
             "s_cols", "s_onehot", "s_index", "s_h", "s_xgT0", "s_out1", "s_silu", "s_xgT1", "s_hT", "s_out0",
             "s_psel", "s_pxt", "s_mm1", "s_pht", "s_mm2"))
        s_ydram = sem("s_ydram")
        s_token = sem("s_token")
        s_x3, s_y = sem("s_x3"), sem("s_y")
        s_yo = [sem("s_yo0"), sem("s_yo1")]
        dve_step, act_step, pool_step = sem("dve_step"), sem("act_step"), sem("pool_step")

        GROUPS = psum_groups(NT, H, KT)
        AT = {key: n for n, (key, _) in enumerate(GROUPS)}
        ORD, seen = {}, {"v": 0, "s": 0}
        for key, e in GROUPS:
            seen[e] += 1
            ORD[key] = (e, seen[e])

        def free_bank(pe, *key):
            g = AT[key]
            if g >= 8:
                e, n = ORD[GROUPS[g - 8][0]]
                pe.wait_ge(drained[e], n)
            return bank[g % 8]

        def full_bank(eng, *key):
            eng.wait_ge(filled, AT[key] + 1)
            return bank[AT[key] % 8]

        def after(eng, *key):
            eng.wait_ge(filled, AT[key] + 1)

        def wait_drained(eng, *key):
            e, n = ORD[key]
            eng.wait_ge(drained[e], n)

        progress = {"v": 0, "s": 0}

        def drain(e, ins, *key):
            progress[e] += 1
            assert ORD[key] == (e, progress[e]), (key, ORD[key], progress[e])
            ins.then_inc(drained[e], 1)

        CH = ["q", "k", "u", "v", "o", "wo0", "wo1", "pj", "gt0", "gt1"]
        wcol0 = {"q": 0, "k": MW, "v": 2 * MW, "o": 3 * MW, "u": 4 * MW + 2 * H}
        LAST = {"q": ("q", 3, 1), "k": ("k", 3, 1), "u": ("u", 3, 1), "v": ("v", 4), "o": ("o", 4),
                "wo0": ("wo", 4, 0), "wo1": ("wo", 4, 1), "pj": ("pj", 4, 1)}

        def chunk(name):
            return ring[:, CH.index(name) % 2, :]

        def chunk_in(eng, name):
            c = CH.index(name)
            eng.wait_ge(s_ring[c % 2], 16 * (c // 2 + 1))

        def bc(dram_row, n=P):
            return dram_row.partition_broadcast(n)

        HG = NEX // 2 * 16
        block = ctx.enter_context(nc.Block())

        @block.sync
        def _(sp):
            xin = [x_prompt[0, P * i:P * i + P, :] for i in range(NP_)] + [x_sample.rearrange("b t d -> (b t) d")]
            sp.dma_start(x[:, 0, :], xin[0]).then_inc(s_x[0], 16)
            sp.dma_start(g_a[:, :], bc(norm_mix_g[0])).then_inc(s_ga, 16)
            for i in range(1, NT):
                sp.dma_start(x[0:ROWS[i], i, :], xin[i]).then_inc(s_x[i], 16)
            wi = w_in[0].rearrange("(p c) n -> p c n", c=KT)
            sp.wait_ge(s_const, 1)
            sp.dma_start(wg[:, :, 0:H], wi[:, :, 4 * MW:4 * MW + H]).then_inc(s_wg, 16)
            sp.dma_start(wg[:, :, 32:32 + H], wi[:, :, 4 * MW + H:4 * MW + 2 * H]).then_inc(s_wg, 16)

            def load_chunk(name):
                c = CH.index(name)
                if c >= 2:
                    after(sp, *LAST[CH[c - 2]])
                if name in wcol0:
                    n0 = wcol0[name]
                    dst, src = chunk(name).rearrange("p (c n) -> p c n", n=512), wi[:, :, n0:n0 + 512]
                elif name[:2] == "wo":
                    n0 = 512 * int(name[2])
                    dst = chunk(name).rearrange("p (c n) -> p c n", n=512)
                    src = w_out[0].rearrange("(c p) n -> p c n", p=P)[:, :, n0:n0 + 512]
                elif name == "pj":
                    dst = chunk(name)[:, 0:2 * DM].rearrange("p (c n) -> p c n", n=DM)
                    src = w_ple_proj[0].rearrange("(c p) n -> p c n", p=P)
                else:
                    n0 = 512 * int(name[2])
                    dst = chunk(name).rearrange("p (c n) -> p c n", n=512)
                    src = w_ple_gate[0].rearrange("(p c) n -> p c n", c=KT)[:, :, n0:n0 + 512]
                sp.dma_start(dst, src).then_inc(s_ring[c % 2], 16)

            load_chunk("q")
            sp.dma_start(gate_b[0:H, :], b_igate.rearrange("a h -> h a"),
                         allow_slow_non_contiguous=True).then_inc(s_small, 16)
            sp.dma_start(gate_b[32:32 + H, :], b_fgate.rearrange("a h -> h a"),
                         allow_slow_non_contiguous=True).then_inc(s_small, 16)
            sp.dma_start(hn_g, head_norm_g[0].rearrange("(h p) -> p h", p=P),
                         allow_slow_non_contiguous=True).then_inc(s_small, 16)
            sp.dma_start(pl_s, pool_scale[0].rearrange("(h p) -> p h", p=P),
                         allow_slow_non_contiguous=True).then_inc(s_small, 16)
            sp.dma_start(m0row, state_m[0].rearrange("b h -> h b"),
                         allow_slow_non_contiguous=True).then_inc(s_small, 16)
            load_chunk("k")
            sp.dma_start(g_b[:, :], bc(norm_ffn_g[0])).then_inc(s_gb, 16)
            sp.dma_start(bufnat, state_pool[0].rearrange("b r c -> (b r) c")).then_inc(s_state, 16)
            sp.dma_start(wp, w_pool[0].rearrange("g c d -> c g d")).then_inc(s_state, 16)
            sp.dma_start(pool_sample[0, :, 0:R - DS, :], state_pool[0, :, DS:R, :]).then_inc(s_stat, 16)
            load_chunk("u")
            load_chunk("v")
            load_chunk("o")
            after(sp, "ps")
            after(sp, "mix", 3, 1)
            for b in range(NB):
                sp.dma_start(C0[:, b, :, 0:P], state_C[0, b].rearrange("h d e -> d h e")).then_inc(s_c0, 16)
            sp.dma_start(n0nat, state_n[0].rearrange("b h d -> (b h) d")).then_inc(s_c0, 16)
            wait_drained(sp, "ps")
            sp.dma_start(pool_prompt[0, 0], ppo).then_inc(s_stat, 16)
            for b in range(NB):
                sp.dma_start(pool_sample[0, b, R - DS:R, :], pso[DS * b:DS * b + DS, :]).then_inc(s_stat, 16)
            load_chunk("wo0")
            load_chunk("wo1")
            sp.dma_start(m_prompt[0].rearrange("a h -> h a"), m_row[:, SEQ - 1:SEQ],
                         allow_slow_non_contiguous=True).then_inc(s_stat, 16)
            sp.dma_start(m_sample[0].rearrange("b h -> h b"), m_row[:, SEQ + DS - 1:T:DS],
                         allow_slow_non_contiguous=True).then_inc(s_stat, 16)
            wait_drained(sp, "Cp", 3)
            sp.dma_start(C_prompt[0, 0].rearrange("h d e -> d h e"), Cp[:, :, 0:P]).then_inc(s_stat, 16)
            wait_drained(sp, "C", 3, 2)
            for b in range(NB):
                sp.dma_start(C_sample[0, b].rearrange("h d e -> d h e"), C0[:, b, :, 0:P]).then_inc(s_stat, 16)
            wait_drained(sp, "nout")
            sp.dma_start(n_sample[0].rearrange("b h d -> (b h) d"), nout[:, 0:P]).then_inc(s_stat, 16)
            sp.dma_start(n_prompt[0, 0], nout[0:H, P:2 * P]).then_inc(s_stat, 16)
            sp.wait_ge(s_stat, 16 * STORES)
            wait_drained(sp, "haT", NT - 1)
            sp.dma_start(rw, router_w[0].rearrange("(p c) e -> p c e", c=KT)).then_inc(s_rt, 16)
            sp.dma_start(rbias, bc(router_bias[0])).then_inc(s_rt, 16)

            def load_expert(j, w1, w3, w2, s13, s2):
                sp.dma_start(w13[j][:, 0], w1.rearrange("(p c) f -> p c f", c=KT)).then_inc(s13, 16)
                sp.dma_start(w13[j][:, 1], w3.rearrange("(p c) f -> p c f", c=KT)).then_inc(s13, 16)
                sp.dma_start(w2s[j], w2.rearrange("(c p) n -> p c n", p=P)).then_inc(s2, 16)

            load_expert(1, sh_w1[0], sh_w3[0], sh_w2[0], s_sh, s_sh)
            for i in range(NP_):
                sp.dma_start(ptile[:, i, :], p_prompt[0, 0, P * i:P * i + P, :]).then_inc(s_p, 16)
            sp.dma_start(ptile[0:NS, NP_, :], p_sample[0].rearrange("b t n -> (b t) n")).then_inc(s_p, 16)
            load_expert(0, ex_w1[0, 0], ex_w3[0, 0], ex_w2[0, 0], s_w13[0], s_w2[0])
            sp.wait_ge(s_xs, NT)
            sp.dma_start(g_a[:, :], bc(norm_ple_g[0])).then_inc(s_ga, 16)
            for i in range(NT):
                if i == NT - 1:
                    load_chunk("pj")
                sp.wait_ge(s_xs, NT + i + 1)
                sp.dma_start(xs_dram[P * i:P * i + ROWS[i], :], xs2[i % 2][0:ROWS[i], :]).then_inc(s_xsd[i % 2], 16)
            sp.dma_start(g_b[:, :], bc(final_norm_g)).then_inc(s_gb, 16)
            load_chunk("gt0")
            for i in range(NT):
                wait_drained(sp, "y", i, 1)
                sp.dma_start(y_dram[P * i:P * i + ROWS[i], :], x[0:ROWS[i], i, :]).then_inc(s_ydram, 16)
            after(sp, "y", NT - 1, 1)
            load_expert(1, ex_w1[0, 1], ex_w3[0, 1], ex_w2[0, 1], s_w13[1], s_w2[1])
            load_chunk("gt1")
            sp.wait_ge(s_np, 1)
            passes = sp.value_load(np_i[0:1, 0:1], min_val=1, max_val=PASSES)

            def load13(m, j, e):
                sp.wait_ge(s_mm1, m - 1)
                for k, w in enumerate((ex_w1, ex_w3)):
                    sp.dma_start(w13[j][:, k], w[0, bass.ds(e, 1)].rearrange("a (p c) f -> p (a c) f", c=KT)
                                 ).then_inc(s_w13[j], 16)

            def load2(m, j, e):
                sp.wait_ge(s_mm2, m - 1)
                sp.dma_start(w2s[j], ex_w2[0, bass.ds(e, 1)].rearrange("a (c p) n -> p (a c) n", p=P)
                             ).then_inc(s_w2[j], 16)

            load13(2, 0, 2)
            with sp.Fori(3, passes * NE - 1, 2) as n:
                for j in range(2):
                    load13(n + j, 1 - j, sp.snap((n + j) % NE))
                    load2(n + (j - 1), j, sp.snap((n + (j - 1)) % NE))
            more = sp.value_load(np_i[0:1, 1:2], min_val=0, max_val=PASSES - 1)
            load13(more * NE + (NE - 1), 1, NE - 1)
            load2(more * NE + (NE - 2), 0, NE - 2)
            load2(more * NE + (NE - 1), 1, NE - 1)
            for b in range(2):
                sp.wait_ge(s_scatter[b], passes * (NE // 2 * 16) + 16)
            for i in range(NT):
                sp.dma_start(x[0:ROWS[i], i, :], y_dram[P * i:P * i + ROWS[i], :]).then_inc(s_x[i], 16)
            yout = [y_prompt[0, P * i:P * i + P, :] for i in range(NP_)] + [y_sample.rearrange("b t d -> (b t) d")]
            for i in range(NT):
                sp.wait_ge(s_y, i + 1)
                sp.dma_start(yout[i], og[i % 2][0:ROWS[i], :]).then_inc(s_yo[i % 2], 16)
            sp.wait_ge(s_yo[0], 16 * 3)
            sp.wait_ge(s_yo[1], 16 * 2)

        @block.gpsimd
        def _(pool):
            n_step = [0]

            def link(ins):
                n_step[0] += 1
                ins.then_inc(pool_step, 1)
                pool.wait_ge(pool_step, n_step[0])

            pool.memset(wg, 0.0).then_inc(s_const, 1)
            pool.memset(eps_c, EPS)
            pool.memset(neg_half, -0.5)
            pool.memset(onesf[:, :], 1.0)
            pool.memset(tri[:, :], 1.0)
            pool.memset(before[:, :], 1.0)
            pool.memset(sel4, 0.0)
            pool.memset(bmask, 1.0)
            pool.memset(keep, 1.0)
            pool.memset(reset, 0.0)
            link(pool.memset(ident[:, :], 0.0))
            pool.affine_select(out=ident[:, :], in_=ident[:, :], compare_op=ALU.not_equal, fill=1.0, base=0,
                               pattern=[[-1, P]], channel_multiplier=1).then_inc(s_const, 1)
            pool.memset(keep[:, SEQ:T:DS], 0.0)
            pool.memset(reset[:, SEQ:T:DS], NEG)
            pool.memset(v[:, :, :, P:DE], 1.0)
            pool.memset(uext[:, :, 0:R], 0.0)
            pool.affine_select(out=tri[:, :], in_=tri[:, :], compare_op=ALU.is_ge, fill=0.0, base=0,
                               pattern=[[1, P]], channel_multiplier=-1)
            pool.affine_select(out=before[:, :], in_=before[:, :], compare_op=ALU.is_ge, fill=0.0, base=-1,
                               pattern=[[1, P]], channel_multiplier=-1)
            pool.affine_select(out=sel4, in_=sel4, compare_op=ALU.not_equal, fill=1.0, base=0,
                               pattern=[[-1, H], [0, P]], channel_multiplier=1)
            link(pool.affine_select(out=bmask[:, 0:NB], in_=bmask[:, 0:NB], compare_op=ALU.is_ge, fill=0.0, base=0,
                                    pattern=[[-DS, NB]], channel_multiplier=1))
            pool.affine_select(out=bmask[:, 0:NB], in_=bmask[:, 0:NB], compare_op=ALU.is_ge, fill=0.0, base=DS - 1,
                               pattern=[[DS, NB]], channel_multiplier=-1)
            bd3 = bd.rearrange("p (b t) -> p b t", t=DS)
            pool.affine_select(out=bd3, in_=tri[0:NS, 0:NS].rearrange("p (b t) -> p b t", t=DS),
                               compare_op=ALU.is_ge, fill=0.0, base=0, pattern=[[-DS, NB], [0, DS]],
                               channel_multiplier=1)
            pool.iota(rcnt_i, pattern=[[0, H], [1, 16]], base=1, channel_multiplier=0)
            pool.iota(toki[:, 0:NT], pattern=[[0, NT]], base=0, channel_multiplier=1)
            pool.iota(toki[:, NT:2 * NT], pattern=[[P, NT]], base=-FAR, channel_multiplier=0)
            link(pool.iota(iotai, pattern=[[1, P]], base=0, channel_multiplier=0))
            pool.tensor_copy(rcnt, rcnt_i)
            pool.tensor_copy(tilef[:, :], toki[:, NT:2 * NT])
            link(pool.tensor_copy(partf[:, :], toki[:, 0:NT]))
            pool.tensor_scalar(binf[:, :], partf[:, 0:1], float(T), None, ALU.add)
            link(pool.tensor_copy(iotaf[:, :], iotai))
            pool.tensor_copy(iotap[:, :], iotaf[:, :]).then_inc(s_const, 1)

            def rms(i, count):
                r = ROWS[i]
                pool.wait_ge(s_sq, count + i + 1)
                link(pool.tensor_scalar(ss[0:r, i:i + 1], ss[0:r, i:i + 1], 1.0 / DM, EPS, ALU.mult, ALU.add))
                pool.tensor_tensor(rstd[0:r, i:i + 1], ss[0:r, i:i + 1], neg_half[0:r, :], ALU.pow
                                   ).then_inc(s_rstd, 1)

            def final_rms(i):
                r = ROWS[i]
                pool.wait_ge(s_sqf, i + 1)
                link(pool.tensor_scalar(ssf[0:r, i:i + 1], ssf[0:r, i:i + 1], 1.0 / DM, EPS, ALU.mult, ALU.add))
                pool.tensor_tensor(rstdf[0:r, i:i + 1], ssf[0:r, i:i + 1], neg_half[0:r, :], ALU.pow
                                   ).then_inc(s_rstdf, 1)

            for i in range(NT):
                rms(i, 0)
            for g in range(H):
                if g == 0:
                    wait_drained(pool, "buf")
                else:
                    pool.wait_ge(s_pooled, g)
                src = uext[:, g, :]
                at = 0
                for k in range(g + 1):
                    w = 1 << k
                    dst = wsum[:, k % 2, :]
                    at += w
                    ins = pool.tensor_tensor(dst[:, at:EXT], src[:, at:EXT], src[:, at - w:EXT - w], ALU.add)
                    if k == g:
                        ins.then_inc(s_wsum, 1)
                    else:
                        link(ins)
                    src = dst
            for h in range(H):
                for j in range(NP_):
                    pool.wait_ge(s_exp, NP_ * h + j + 1)
                    blk = D[:, BLK[j]:BLK[j] + P]
                    ins = pool.tensor_tensor(blk, blk, tri[:, :], ALU.mult)
                    link(ins)
                    pool.tensor_copy(wcol[:, j, h:h + 1], D[:, BLK[j + 1] - 1:BLK[j + 1]]).then_inc(s_msk, 1)
            pool.wait_ge(s_exps, 1)
            pool.tensor_tensor(Ds, Ds, bd.unsqueeze(1).to_broadcast([NS, H, NS]), ALU.mult).then_inc(s_msks, 1)
            for n, (r, i0, i1) in enumerate(((P, 0, NP_), (NS, NP_, NT))):
                pool.wait_ge(s_var, n + 1)
                nh = neg_half[0:r, :].unsqueeze(2).to_broadcast([r, i1 - i0, H])
                pool.tensor_tensor(fac[0:r, 3, i0:i1, :], fac[0:r, 2, i0:i1, :], nh, ALU.pow).then_inc(s_pw, 1)
            wait_drained(pool, "haT", NT - 1)
            pool.wait_ge(s_stat, 16 * STORES)
            link(pool.memset(lower, 1.0))
            pool.affine_select(out=lower, in_=lower, compare_op=ALU.is_ge, fill=0.0, base=-1,
                               pattern=[[1, NG], [-1, NG]], channel_multiplier=0)
            link(pool.memset(table[:, :, :], 0.0))
            pool.memset(tplace[:, NE:TE, :], -1.0)
            pool.tensor_copy(tpick[:, :, :, 0], partf[:, :].unsqueeze(1).to_broadcast([P, TE, NT]))
            pool.tensor_copy(tpick[:, :, :, 1], tilef[:, :].unsqueeze(1).to_broadcast([P, TE, NT])
                             ).then_inc(s_const, 1)
            for i in range(NT):
                rms(i, NT)

            for k in range(2):
                pool.wait_ge(s_xsd[k], 16 * (3 - k))
            after(pool, "x2T", NT - 1, 1)
            pool.memset(xg[0], 0.0)
            link(pool.memset(xg[1], 0.0))
            for b in range(2):
                pool.dma_start(y_dram[T + P // 2 * b:T + P // 2 * (b + 1), :], xg[b][0:P // 2, :]
                               ).then_inc(s_scatter[b], 16)
            for b in range(2):
                pool.wait_ge(s_scatter[b], 16)
            pool.wait_ge(s_ydram, 16 * NT)

            def wait_on_its_own():
                pool.sem_inc(s_carried, 1)

            def gather(base, n, k, b):
                pool.wait_ge(s_index, base + n)
                wait_on_its_own()
                pool.indirect_dma_start(xg[b], None, xs_dram,
                                        bass.IndirectOffsetOnAxis(slot[k][:, 0:1], 0),
                                        bounds_check=T - 1, oob_is_err=False).then_inc(s_gather[b], 16)

            pool.wait_ge(s_np, 1)
            passes = pool.value_load(np_i[0:1, 0:1], min_val=1, max_val=PASSES)
            with pool.Fori(0, passes, 1) as r:
                gather(r * NEX, 1, 0, 0)
                gather(r * NEX, 2, 1, 1)

                def scatter(n, j):
                    b = (j + 1) % 2
                    pool.wait_ge(s_out0, r * NE + n + j)
                    pool.wait_ge(s_out1, r * NE + n + j)
                    pool.wait_ge(s_scatter[1 - b], r * (NE // 2 * 16) + n * 8 + (1 + j // 2) * 16)
                    wait_on_its_own()
                    pool.indirect_dma_start(y_dram, bass.IndirectOffsetOnAxis(outrow[b][:, 0:1], 0),
                                            og[b], None, compute_op=ALU.add).then_inc(s_scatter[b], 16)

                def step(n, j, first=False):
                    pool.wait_ge(s_pxt, r * (NE + 1) + n + (j + 1))
                    gather(r * NEX + n, j + 3, (j + 2) % 4, j % 2)
                    if not first:
                        scatter(n, j)

                for j in range(4):
                    step(0, j, j == 0)
                with pool.Fori(4, NE, 4) as n:
                    for j in range(4):
                        step(n, j)
                scatter(NE, 0)
                pool.wait_ge(s_pxt, (r + 1) * (NE + 1))
            for i in range(4):
                rms(i, 2 * NT)
            final_rms(0)
            rms(4, 2 * NT)
            for i in range(1, NT):
                final_rms(i)

        @block.scalar
        def _(act):
            def square(i, n):
                r = ROWS[i]
                act.activation(junk[0:r, :], x[0:r, i, :], ACT.Square, accum_out=ss[0:r, i:i + 1]).then_inc(s_sq, 1)
                act.wait_ge(s_sq, n)

            for i in range(NT + 1):
                if i < NT:
                    act.wait_ge(s_x[i], 16)
                    square(i, i + 1)
                if i >= 1:
                    b = full_bank(act, "x1T", i - 1, 1)
                    r = ROWS[i - 1]
                    drain("s", act.copy(xT[:, 4:8, tok(i - 1)], b[:, :].rearrange("p (c t) -> p c t", t=P)[:, :, 0:r]),
                          "x1T", i - 1, 1)
            act.wait_ge(s_abs, 1)
            act.activation(r_e, r_e, ACT.Exp, scale=-1.0).then_inc(act_step, 1)
            act.wait_ge(act_step, 1)
            act.activation(r_l, r_e, ACT.Ln, bias=1.0).then_inc(s_ln, 1)
            for j in range(H):
                for n in range(2):
                    b = full_bank(act, "q", j, n)
                    drain("s", act.mul(qT[:, j, TH * n:TH * n + TH], b[:, 0:TH], float(P) ** -0.5), "q", j, n)
            act.wait_ge(s_mrow, 1)
            act.activation(em_row, m_row, ACT.Exp, scale=-1.0)
            act.activation(srow[:, NS:2 * NS + NB], srow[:, NS:2 * NS + NB], ACT.Exp).then_inc(s_em, 1)
            for j in range(H):
                for n in range(2):
                    b = full_bank(act, "k", j, n)
                    drain("s", act.copy(kT[:, j, TH * n:TH * n + TH], b[:, 0:TH]), "k", j, n)
            act.wait_ge(s_small, 16 * 5)
            for j in range(H):
                for n in range(2):
                    b = full_bank(act, "mix", j, n)
                    drain("s", act.activation(mixT[:, H + j, TH * n:TH * n + TH], b[:, 0:TH], ACT.Copy,
                                              scale=pl_s[:, j:j + 1]), "mix", j, n)
            b = full_bank(act, "pp")
            drain("s", act.copy(ppo, b[0:R, :]), "pp")
            b = full_bank(act, "ps")
            drain("s", act.copy(pso, b[0:NS, :]), "ps")
            for h in range(H):
                for j in range(NP_):
                    act.wait_ge(s_dif, NP_ * h + j + 1)
                    blk = D[:, BLK[j]:BLK[j + 1]]
                    act.activation(blk, blk, ACT.Exp, scale=-1.0).then_inc(s_exp, 1)
                b = full_bank(act, "o", h)
                drain("s", act.activation(so[:, h, :], b[:, :], ACT.Tanh, scale=0.5), "o", h)
                for i in range(NP_):
                    b = full_bank(act, "num", h, i)
                    drain("s", act.copy(nb[:, i, h, :], b[:, 0:DE]), "num", h, i)
            wait_drained(act, "num", H - 1, NP_ - 1)
            for i in range(NP_):
                for h in range(H):
                    ins = act.activation(junk[:, 0:P], nb[:, i, h, 0:P], ACT.Square, accum_out=fac[:, 0, i, h:h + 1])
                    ins.then_inc(s_sqh, 1)
                    act.wait_ge(s_sqh, H * i + h + 1)
            act.wait_ge(s_difs, 1)
            act.activation(Ds, Ds, ACT.Exp, scale=-1.0).then_inc(s_exps, 1)
            for h in range(H):
                b = full_bank(act, "Cp", h)
                drain("s", act.copy(Cp[:, h, :], b[:, 0:DE]), "Cp", h)
            b = full_bank(act, "kns")
            drain("s", act.copy(kws, b[0:NS, :].rearrange("p (h d) -> p h d", d=P)), "kns")
            b = full_bank(act, "o", 4)
            drain("s", act.activation(so[0:NS, 4, :], b[0:NS, :], ACT.Tanh, scale=0.5), "o", 4)
            b = full_bank(act, "nT")
            drain("s", act.copy(numT, b[:, 0:H * NS].rearrange("p (h t) -> p h t", t=NS)), "nT")
            b = full_bank(act, "nTt")
            drain("s", act.copy(nb[0:NS, NP_, :, 0:P], b[0:NS, :].rearrange("p (h d) -> p h d", d=P)), "nTt")
            wait_drained(act, "nTt")
            for h in range(H):
                ins = act.activation(junk[0:NS, 0:P], nb[0:NS, NP_, h, 0:P], ACT.Square,
                                     accum_out=fac[0:NS, 0, NP_, h:h + 1])
                ins.then_inc(s_sqh, 1)
                act.wait_ge(s_sqh, H * NP_ + h + 1)
            b = full_bank(act, "nout")
            act.copy(nout[:, 0:P], b[0:NB * H, 0:P])
            drain("s", act.copy(nout[0:H, P:2 * P], b[0:H, P:2 * P]), "nout")

            def square2(i):
                act.wait_ge(s_x1, i + 1)
                square(i, NT + i + 1)

            def x2t(i):
                r = ROWS[i]
                b = full_bank(act, "x2T", i, 1)
                drain("s", act.copy(xT[:, 4:8, tok(i)], b[:, :].rearrange("p (c t) -> p c t", t=P)[:, :, 0:r]),
                      "x2T", i, 1)
                b = full_bank(act, "r", i)
                drain("s", act.activation(sc_[0:r, i, :], b[0:r, 0:NE], ACT.Tanh, scale=0.5), "r", i)
                b = full_bank(act, "sh", i)
                if i:
                    act.wait_ge(s_hsh, i)
                act.activation(hs[0:r, :], b[0:r, 0:FF], ACT.Silu).then_inc(s_silu_sh, 1)

            def sht(i):
                r = ROWS[i]
                b = full_bank(act, "shT", i)
                drain("s", act.copy(hT[:, :, 0:r], b[:, 0:2 * P].rearrange("p (c t) -> p c t", t=P)[:, :, 0:r]),
                      "shT", i)

            wait_drained(act, "haT", NT - 1)
            act.wait_ge(s_stat, 16 * STORES)
            square2(0)
            square2(1)
            x2t(0)
            square2(2)
            sht(0)
            x2t(1)
            square2(3)
            sht(1)
            x2t(2)
            square2(4)
            sht(2)
            x2t(3)
            for i in range(NT):
                b = full_bank(act, "pT", i)
                r = ROWS[i]
                drain("s", act.copy(pT[:, :, tok(i)], b[:, 0:2 * P].rearrange("p (c t) -> p c t", t=P)[:, :, 0:r]),
                      "pT", i)
            sht(3)
            x2t(4)

            def pj(i):
                r = ROWS[i]
                for n in range(2):
                    b = full_bank(act, "pj", i, n)
                    drain("s", act.copy(proj[0:r, i, 512 * n:512 * n + 512], b[0:r, :]), "pj", i, n)

            pj(0)
            pj(1)
            sht(4)
            for i in range(2, NT):
                pj(i)

            def xg_half(base, n, b):
                act.wait_ge(s_pxt, base + n)
                act.copy(xgT[b][:, 4:8, :], bank[1][:, :].rearrange("p (c t) -> p c t", t=P)).then_inc(s_xgT1, 1)

            act.wait_ge(s_np, 1)
            passes = act.value_load(np_i[0:1, 0:1], min_val=1, max_val=PASSES)
            with act.Fori(0, passes, 1) as r:
                xg_half(r * (NE + 1), 1, 0)

                def out(n, j):
                    b = (j + 1) % 2
                    act.wait_ge(s_mm2, r * NE + n + j)
                    act.wait_ge(s_scatter[b], r * (NE // 2 * 16) + n * 8 + (j + 1) // 2 * 16)
                    act.copy(og[b][:, 0:512], bank[5][:, :]).then_inc(s_out0, 1)

                def step(n, j, first=False):
                    act.wait_ge(s_mm1, r * NE + n + (j + 1))
                    act.activation(hs, bank[2][:, 0:FF], ACT.Silu).then_inc(s_silu, 1)
                    xg_half(r * (NE + 1) + n, j + 2, (j + 1) % 2)
                    if not first:
                        out(n, j)
                    act.wait_ge(s_pht, r * NE + n + (j + 1))
                    act.copy(hT, bank[4][:, 0:2 * P].rearrange("p (c t) -> p c t", t=P)).then_inc(s_hT, 1)

                for j in range(4):
                    step(0, j, j == 0)
                with act.Fori(4, NE, 4) as n:
                    for j in range(4):
                        step(n, j)
                out(NE, 0)
                act.wait_ge(s_xgT1, (r + 1) * (NE + 1))

            def square3(i):
                act.wait_ge(s_x[i], 32)
                square(i, 2 * NT + i + 1)

            def final_square(i):
                r = ROWS[i]
                act.wait_ge(s_x3, i + 1)
                act.activation(junk[0:r, :], x[0:r, i, :], ACT.Square, accum_out=ssf[0:r, i:i + 1]).then_inc(s_sqf, 1)
                act.wait_ge(s_sqf, i + 1)

            def gates(i):
                r = ROWS[i]
                for n in range(2):
                    b = full_bank(act, "gt", i, n)
                    if i >= 2 and n == 0:
                        act.wait_ge(s_x3, i - 1)
                    drain("s", act.activation(gsig[i % 2][0:r, 512 * n:512 * n + 512], b[0:r, :], ACT.Tanh,
                                              scale=0.5), "gt", i, n)

            square3(0)
            for i in range(NT):
                r = ROWS[i]
                if i + 1 < NT:
                    square3(i + 1)
                b = full_bank(act, "x3T", i, 1)
                drain("s", act.copy(xT[:, 4:8, tok(i)], b[:, :].rearrange("p (c t) -> p c t", t=P)[:, :, 0:r]),
                      "x3T", i, 1)
                if i:
                    gates(i - 1)
                if i >= 2:
                    final_square(i - 2)
            gates(NT - 1)
            final_square(NT - 2)
            final_square(NT - 1)

        @block.vector
        def _(dve):
            n_step = [0]

            def link(ins):
                n_step[0] += 1
                ins.then_inc(dve_step, 1)
                dve.wait_ge(dve_step, n_step[0])

            def swizzled(row, r):
                return row[0:r, :].rearrange("t (c p) -> t p c", p=P)

            def normalise(i, dst, g, count):
                r = ROWS[i]
                dve.wait_ge(s_rstd, count + i + 1)
                dve.scalar_tensor_tensor(out=swizzled(dst, r), in0=x[0:r, i, :].rearrange("t (p c) -> t p c", c=KT),
                                         scalar=rstd[0:r, i:i + 1],
                                         in1=g[0:r, :].rearrange("t (p c) -> t p c", c=KT),
                                         op0=ALU.mult, op1=ALU.mult).then_inc(s_xs, 1)

            def turned(key, i):
                b = full_bank(dve, key, i, 0)
                r = ROWS[i]
                drain("v", dve.tensor_copy(xT[:, 0:4, tok(i)],
                                           b[:, :].rearrange("p (c t) -> p c t", t=P)[:, :, 0:r]), key, i, 0)

            dve.wait_ge(s_ga, 16)
            for i in range(NT + 1):
                if i < NT:
                    if i >= 2:
                        after(dve, "x1T", i - 2, 1)
                    normalise(i, xs1[:, i % 2, :], g_a, 0)
                if i >= 1:
                    turned("x1T", i - 1)
            dve.wait_ge(s_small, 16 * 5)
            for n in range(2):
                b = full_bank(dve, "g", n)
                c = slice(TH * n, TH * n + TH)
                dve.tensor_scalar(r_i[:, c], b[0:H, 0:TH], gate_b[0:H, :], None, ALU.add)
                drain("v", dve.tensor_scalar(r_f[:, c], b[32:32 + H, 0:TH], gate_b[32:32 + H, :], None, ALU.add),
                      "g", n)
            wait_drained(dve, "g", 1)
            dve.scalar_tensor_tensor(out=r_e, in0=r_f, scalar=-1.0, in1=r_f, op0=ALU.mult, op1=ALU.max
                                     ).then_inc(s_abs, 1)
            dve.wait_ge(s_ln, 1)
            link(dve.scalar_tensor_tensor(out=r_l, in0=r_f, scalar=0.0, in1=r_l, op0=ALU.min, op1=ALU.subtract))
            dve.wait_ge(s_const, 3)
            link(dve.tensor_tensor_scan(r_e, keep, r_l, 0.0, ALU.mult, ALU.add))
            link(dve.tensor_tensor(a_row, r_i, r_e, ALU.subtract))
            link(dve.tensor_copy(r_f, a_row))
            link(dve.tensor_tensor(r_f[:, SEQ:T:DS], a_row[:, SEQ:T:DS], m0row, ALU.max))
            link(dve.tensor_tensor_scan(M_row, reset, r_f, 0.0, ALU.add, ALU.max))
            dve.tensor_tensor(m_row, r_e, M_row, ALU.add)
            dve.tensor_copy(srow[:, 0:NS], M_row[:, SEQ:T])
            m0b = m0row.unsqueeze(2).to_broadcast([H, NB, DS])
            dve.tensor_tensor(srow[:, NS:2 * NS].rearrange("p (b t) -> p b t", t=DS), m0b,
                              M_row[:, SEQ:T].rearrange("p (b t) -> p b t", t=DS), ALU.subtract)
            dve.tensor_tensor(srow[:, 2 * NS:2 * NS + NB], m0row, M_row[:, SEQ + DS - 1:T:DS], ALU.subtract
                              ).then_inc(s_mrow, 1)
            for g in range(H):
                dve.tensor_scalar(rcnt[:, g, :], rcnt[:, g, :], float(WINDOWS[g]), None, ALU.min)
            link(dve.memset(small[0:1, 30:31], 0.0))
            dve.reciprocal(rcnt, rcnt)
            dve.wait_ge(s_const, 3)
            for j in range(H):
                for n in range(2):
                    b = full_bank(dve, "u", j, n)
                    if n == 0:
                        ins = dve.tensor_copy(uext[:, j, R:R + TH], b[:, 0:TH])
                    else:
                        dve.tensor_copy(uext[:, j, R + TH:SEGP], b[:, 0:SEQ - TH])
                        dve.tensor_copy(us[:, j, :], b[:, SEQ - TH:TH])
                        ins = dve.tensor_copy(uext[:, j, SEGP:EXT].rearrange("p (b t) -> p b t", t=SEGS)[:, :, R:SEGS],
                                              b[:, SEQ - TH:TH].rearrange("p (b t) -> p b t", t=DS))
                    drain("v", ins, "u", j, n)
            b = full_bank(dve, "buf")
            for j in range(H):
                ins = dve.tensor_copy(uext[:, j, SEGP:EXT].rearrange("p (b t) -> p b t", t=SEGS)[:, :, 0:R],
                                      b[:, P * j:P * j + NB * R].rearrange("p (b t) -> p b t", t=R))
            drain("v", ins, "buf")
            link(dve.memset(small[0:1, 30:31], 0.0))

            def pooling(g):
                w = WINDOWS[g]
                win = wsum[:, g % 2, :]
                dst = pooled[:, g % 2, :]
                dve.wait_ge(s_wsum, g + 1)
                if g >= 2:
                    after(dve, "mix", g - 2, 1)
                dve.scalar_tensor_tensor(out=dst[:, 16:SEQ], in0=win[:, R + 16:SEGP], scalar=1.0 / w,
                                         in1=uext[:, g, R + 16:SEGP], op0=ALU.mult, op1=ALU.subtract)
                seg = slice(SEGP, EXT)
                dve.scalar_tensor_tensor(
                    out=dst[:, SEQ:T].rearrange("p (b t) -> p b t", t=DS),
                    in0=win[:, seg].rearrange("p (b t) -> p b t", t=SEGS)[:, :, R:SEGS], scalar=1.0 / w,
                    in1=uext[:, g, seg].rearrange("p (b t) -> p b t", t=SEGS)[:, :, R:SEGS],
                    op0=ALU.mult, op1=ALU.subtract)
                link(dve.tensor_tensor(dst[:, 0:16], win[:, R:R + 16], rcnt[:, g, :], ALU.mult))
                dve.tensor_tensor(dst[:, 0:16], dst[:, 0:16], uext[:, g, R:R + 16], ALU.subtract
                                  ).then_inc(s_pooled, 1)

            for i in range(NT):
                b = full_bank(dve, "v", i)
                r = ROWS[i]
                drain("v", dve.tensor_copy(v[0:r, i, :, 0:P], b[0:r, :].rearrange("p (h d) -> p h d", d=P)), "v", i)
                if i < 2:
                    pooling(i)
            b = full_bank(dve, "nat")
            nat = b[:, 0:2 * NT * H].rearrange("p (a i h) -> p a i h", i=NT, h=H)
            dve.tensor_copy(anat[:, :, 0:NP_, :], nat[:, :, 0:NP_, :])
            drain("v", dve.tensor_copy(anat[0:NS, :, NP_, :], nat[0:NS, :, NP_, :]), "nat")
            wait_drained(dve, "nat")
            pooling(2)
            pooling(3)
            for h in range(H):
                b = full_bank(dve, "Mb", h)
                if h:
                    dve.wait_ge(s_pt, NP_ * h)
                    dve.wait_ge(s_msk, NP_ * h)
                for j in range(NP_):
                    dve.tensor_scalar(D[:, BLK[j]:BLK[j + 1]], b[:, P * j:SEQ], anat[:, 0, j, h:h + 1], 0.0,
                                      ALU.subtract, ALU.max).then_inc(s_dif, 1)
                dve.wait_ge(s_dif, NP_ * h + NP_)
                drain("v", dve.memset(small[0:1, 30:31], 0.0), "Mb", h)
                if h:
                    after(dve, "num", h - 1, NP_ - 1)
                for j in range(NP_):
                    b = full_bank(dve, "S", h, j)
                    dve.wait_ge(s_msk, NP_ * h + j + 1)
                    drain("v", dve.tensor_tensor(PT[:, BLK[j]:BLK[j + 1]], b[:, 0:SEQ - P * j],
                                                 D[:, BLK[j]:BLK[j + 1]], ALU.mult), "S", h, j)
                wait_drained(dve, "S", h, NP_ - 1)
                dve.memset(small[0:1, 30:31], 0.0).then_inc(s_pt, NP_)
            def factors(n, r, i0, i1):
                f = [fac[0:r, k, i0:i1, :] for k in range(6)]
                nq = nb[0:r, i0:i1, :, P]
                link(dve.scalar_tensor_tensor(out=f[4], in0=nq, scalar=-1.0, in1=nq, op0=ALU.mult, op1=ALU.max))
                link(dve.tensor_tensor(f[4], f[4], anat[0:r, 1, i0:i1, :], ALU.max))
                link(dve.reciprocal(f[1], f[4]))
                dve.wait_ge(s_sqh, H * i1)
                link(dve.tensor_tensor(f[2], f[0], f[1], ALU.mult))
                link(dve.tensor_tensor(f[2], f[2], f[1], ALU.mult))
                dve.tensor_scalar(f[2], f[2], 1.0 / P, EPS, ALU.mult, ALU.add).then_inc(s_var, 1)
                dve.wait_ge(s_pw, n + 1)
                link(dve.scalar_tensor_tensor(out=f[5], in0=f[3], scalar=0.5, in1=f[1], op0=ALU.mult, op1=ALU.mult))

            for k in range(2):
                b = full_bank(dve, "Ms", k)
                ms = b[:, 0:2 * (2 * NS + NB)].rearrange("p (h n) -> p h n", h=2)
                hh2 = slice(2 * k, 2 * k + 2)
                dve.tensor_tensor(Ds[:, hh2, :], ms[0:NS, :, 0:NS],
                                  anat[0:NS, 0, NP_, hh2].unsqueeze(2).to_broadcast([NS, 2, NS]), ALU.subtract)
                dve.tensor_tensor(qw[:, hh2, :], ms[:, :, NS:2 * NS], qT[:, hh2, SEQ:T], ALU.mult)
                drain("v", dve.tensor_copy(fwb[:, hh2, :], ms[:, :, 2 * NS:2 * NS + NB]), "Ms", k)
            wait_drained(dve, "Ms", 1)
            dve.tensor_scalar(Ds, Ds, 0.0, None, ALU.max).then_inc(s_difs, 1)
            b = full_bank(dve, "Ss")
            dve.wait_ge(s_msks, 1)
            drain("v", dve.tensor_tensor(PTs, b[0:NS, 0:H * NS].rearrange("p (h t) -> p h t", t=NS), Ds, ALU.mult), "Ss")
            for h in range(H):
                b = full_bank(dve, "kn", h)
                if h >= 2:
                    after(dve, "Cp", h - 2)
                drain("v", dve.tensor_tensor(kw[:, h % 2], b[:, :].rearrange("p (j d) -> p j d", d=P),
                                             wcol[:, :, h:h + 1].to_broadcast([P, NP_, P]), ALU.mult), "kn", h)
            wait_drained(dve, "num", H - 1, NP_ - 1)
            factors(0, P, 0, NP_)
            b = full_bank(dve, "n0")
            dve.wait_ge(s_c0, 16 * (NB + 1))
            drain("v", dve.tensor_copy(C0[:, :, :, P], b[:, 0:NB * H].rearrange("p (b h) -> p b h", h=H)), "n0")
            b = full_bank(dve, "nqs")
            ins = dve.tensor_tensor(nq9, b[0:NS, 0:16 * H].rearrange("p (h c) -> p h c", c=16)[:, :, 0:NB + 1],
                                    bmask.unsqueeze(1).to_broadcast([NS, H, NB + 1]), ALU.mult)
            drain("v", ins, "nqs")
            wait_drained(dve, "nqs")
            link(dve.tensor_reduce(nb[0:NS, NP_, :, P], nq9, AX.X, ALU.add))
            for h in range(H):
                if h:
                    after(dve, "C", h - 1, 2)
                dve.tensor_tensor(Vb[0:NS], v[0:NS, NP_, h, :].unsqueeze(1).to_broadcast([NS, NB, DE]),
                                  Ds[:, h, DS - 1:NS:DS].unsqueeze(2).to_broadcast([NS, NB, DE]), ALU.mult
                                  ).then_inc(s_vb, 1)
                for c in range(3):
                    b = full_bank(dve, "C", h, c)
                    for k in range(3 * c, min(3 * c + 3, NB)):
                        ins = dve.scalar_tensor_tensor(out=C0[:, k, h, :], in0=C0[:, k, h, :],
                                                       scalar=fwb[:, h, k:k + 1],
                                                       in1=b[:, DE * (k - 3 * c):DE * (k - 3 * c + 1)],
                                                       op0=ALU.mult, op1=ALU.add)
                    drain("v", ins, "C", h, c)
            wait_drained(dve, "nTt")
            factors(1, NS, NP_, NT)

            def turn_ha(i):
                b = full_bank(dve, "haT", i)
                r = ROWS[i]
                drain("v", dve.tensor_tensor(
                    mixT[:, 0:H, tok(i)], b[:, :].rearrange("p (h t) -> p h t", t=P)[:, :, 0:r],
                    hn_g.unsqueeze(2).to_broadcast([P, H, r]), ALU.mult), "haT", i)

            for i in range(NT):
                r = ROWS[i]
                if i >= 2:
                    after(dve, "haT", i - 2)
                wait_drained(dve, "o", i)
                hb = ha[0:r, i % 2, :]
                link(dve.tensor_tensor(hb.rearrange("p (h d) -> p h d", d=P), nb[0:r, i, :, 0:P],
                                       fac[0:r, 5, i, :].unsqueeze(2).to_broadcast([r, H, P]), ALU.mult))
                dve.scalar_tensor_tensor(out=hb, in0=so[0:r, i, :], scalar=1.0, in1=hb, op0=ALU.add, op1=ALU.mult
                                         ).then_inc(s_ha, 1)
                if i:
                    turn_ha(i - 1)
            turn_ha(NT - 1)

            dve.wait_ge(s_gb, 16)
            dve.wait_ge(s_stat, 16 * STORES)

            def add_x(key, i):
                r = ROWS[i]
                for n in range(2):
                    b = full_bank(dve, key, i, n)
                    c = slice(512 * n, 512 * n + 512)
                    drain("v", dve.tensor_tensor(x[0:r, i, c], b[0:r, :], x[0:r, i, c], ALU.add), key, i, n)
                wait_drained(dve, key, i, 1)

            def x1(i):
                add_x("wo", i)
                dve.memset(small[0:1, 30:31], 0.0).then_inc(s_x1, 1)

            def norm2(i):
                if i >= 2:
                    after(dve, "x2T", i - 2, 1)
                    dve.wait_ge(s_xsd[i % 2], 16 * (i // 2))
                normalise(i, xs2[i % 2], g_b, NT)

            def x2t(i):
                turned("x2T", i)
                r = ROWS[i]
                dve.wait_ge(s_silu_sh, i + 1)
                b = full_bank(dve, "sh", i)
                if i:
                    after(dve, "shT", i - 1)
                drain("v", dve.tensor_tensor(hh[0:r, :], b[0:r, FF:2 * FF], hs[0:r, :], ALU.mult), "sh", i)
                wait_drained(dve, "sh", i)
                dve.memset(small[0:1, 30:31], 0.0).then_inc(s_hsh, 1)

            x1(0)
            norm2(0)
            x1(1)
            norm2(1)
            x2t(0)
            x1(2)
            norm2(2)
            add_x("y", 0)
            x2t(1)
            x1(3)
            norm2(3)
            add_x("y", 1)
            x2t(2)
            x1(4)
            norm2(4)
            add_x("y", 2)
            x2t(3)
            add_x("y", 3)
            x2t(4)

            wait_drained(dve, "r", NT - 1)
            dve.wait_ge(s_rt, 32)
            link(dve.memset(sc_[NS:P, NP_, :], 0.0))
            link(dve.tensor_scalar(sc_, sc_, 0.5, 0.5, ALU.mult, ALU.add))
            link(dve.tensor_tensor(bi_, sc_, rbias.unsqueeze(1).to_broadcast([P, NT, NE]), ALU.add))
            g4 = [gs_[:, k] for k in range(8)]

            def by_group(t):
                return t.rearrange("p i (g k) -> p (i g) k", k=NG)

            def flat(t):
                return t.rearrange("p i g -> p (i g)")

            def spread(t, k=NG):
                return flat(t).unsqueeze(2).to_broadcast([P, NT * NG, k])

            link(dve.tensor_reduce(flat(g4[0]), by_group(bi_), AX.X, ALU.max))
            link(dve.tensor_tensor(by_group(t1_), by_group(bi_), spread(g4[0]), ALU.is_equal))
            link(dve.tensor_reduce(flat(g4[1]), by_group(t1_), AX.X, ALU.add))
            link(dve.scalar_tensor_tensor(out=t2_.rearrange("p i e -> p (i e)"),
                                          in0=t1_.rearrange("p i e -> p (i e)"), scalar=NEG,
                                          in1=bi_.rearrange("p i e -> p (i e)"), op0=ALU.mult, op1=ALU.add))
            link(dve.tensor_reduce(flat(g4[2]), by_group(t2_), AX.X, ALU.max))
            link(dve.tensor_scalar(g4[1], g4[1], 1.5, NEG, ALU.is_lt, ALU.mult))
            link(dve.tensor_tensor(g4[1], g4[1], g4[0], ALU.add))
            link(dve.tensor_tensor(g4[2], g4[2], g4[1], ALU.max))
            link(dve.tensor_tensor(g4[3], g4[0], g4[2], ALU.add))
            dve.wait_ge(s_const, 4)
            for i in range(NT):
                s = g4[3][:, i, :]
                row_a = s.unsqueeze(2).to_broadcast([P, NG, NG])
                row_b = s.unsqueeze(1).to_broadcast([P, NG, NG])
                ta = t1_[:, i, :].rearrange("p (a b) -> p a b", b=NG)
                tb = t2_[:, i, :].rearrange("p (a b) -> p a b", b=NG)
                dve.tensor_tensor(ta, row_b, row_a, ALU.is_gt)
                dve.tensor_tensor(tb, row_b, row_a, ALU.is_equal)
            link(dve.memset(small[0:1, 30:31], 0.0))
            low5 = lower.rearrange("p a b -> p (a b)").unsqueeze(1).to_broadcast([P, NT, NE])
            link(dve.tensor_tensor(t2_, t2_, low5, ALU.mult))
            link(dve.tensor_tensor(t1_, t1_, t2_, ALU.add))
            link(dve.tensor_reduce(flat(g4[4]), by_group(t1_), AX.X, ALU.add))
            link(dve.tensor_scalar(g4[5], g4[4], 3.5, None, ALU.is_lt))
            link(dve.tensor_scalar(g4[6], g4[5], -1.0, -NEG, ALU.add, ALU.mult))
            link(dve.tensor_tensor(by_group(t1_), by_group(bi_), spread(g4[5]), ALU.mult))
            link(dve.tensor_tensor(by_group(t1_), by_group(t1_), spread(g4[6]), ALU.add))
            for i in range(NT):
                dve.max(top[:, i, :], t1_[:, i, :])
            link(dve.memset(small[0:1, 30:31], 0.0))
            for i in range(NT):
                dve.match_replace(out=t2_[:, i, :], in_to_replace=top[:, i, :], in_values=t1_[:, i, :],
                                  imm_value=2 * NEG)
            link(dve.memset(small[0:1, 30:31], 0.0))
            link(dve.tensor_tensor(sel_, t1_, t2_, ALU.not_equal))
            link(dve.tensor_tensor(gt_, sc_, sel_, ALU.mult))
            link(dve.tensor_reduce(g4[7][:, :, 0], gt_, AX.X, ALU.add))
            link(dve.reciprocal(g4[7][:, :, 1], g4[7][:, :, 0]))
            link(dve.memset(sel_[NS:P, NP_, :], 0.0))
            dve.memset(small[0:1, 30:31], 0.0).then_inc(s_sel0, 1)
            link(dve.tensor_tensor(gt_, gt_, g4[7][:, :, 1:2].to_broadcast([P, NT, NE]), ALU.mult))
            add_x("y", 4)
            link(dve.tensor_scalar(gt_, gt_, ROUTED_SCALE, None, ALU.mult))
            for k in range(3):
                part = tpick[:, 0:NE, :, 2 + k].rearrange("p e i -> p i e")
                link(dve.tensor_copy(part, gt_))
                if k < 2:
                    link(dve.tensor_tensor(gt_, gt_, part, ALU.subtract))
            b = full_bank(dve, "pos")
            pos = b[:, 0:NT * NE].rearrange("p (i e) -> p i e", e=NE)
            dve.tensor_scalar(t1_, pos, 1.0, None, ALU.add)
            drain("v", dve.tensor_reduce(np_f[0:1, 0:1], b[0:1, NT * NE:(NT + 1) * NE], AX.X, ALU.max), "pos")
            wait_drained(dve, "pos")
            link(dve.tensor_tensor(t1_, t1_, sel_, ALU.mult))
            link(dve.tensor_scalar(tplace[:, 0:NE, :].rearrange("p e i -> p i e"), t1_, -1.0, None, ALU.add))
            link(dve.tensor_scalar(np_f[0:1, 1:2], np_f[0:1, 0:1], P + 0.5, 1.0, ALU.is_gt, ALU.add))
            for k in range(2, PASSES):
                link(dve.tensor_scalar(np_f[0:1, 2:3], np_f[0:1, 0:1], k * P + 0.5, None, ALU.is_gt))
                link(dve.tensor_tensor(np_f[0:1, 1:2], np_f[0:1, 1:2], np_f[0:1, 2:3], ALU.add))
            dve.tensor_scalar(np_i[0:1, 1:2], np_f[0:1, 1:2], -1.0, None, ALU.add)
            dve.tensor_copy(np_i[0:1, 0:1], np_f[0:1, 1:2]).then_inc(s_np, 1)
            def one_hot(base, n, b, e):
                dve.tensor_copy(cols[b], table[:, bass.ds(e, 1), :].rearrange("p a c -> p (a c)")
                                ).then_inc(s_cols, 1)
                dve.wait_ge(s_cols, base + n)
                for i in range(NT):
                    ins = dve.tensor_scalar(onehot[b][:, i, :], iotap[:, :], place5[b][:, i:i + 1], None, ALU.is_equal)
                ins.then_inc(s_onehot, 1)

            def index(base, n, k):
                dve.wait_ge(s_psel, base + n)
                dve.tensor_reduce(token[k % 2][:, :], bank[7][:, 0:2], AX.X, ALU.add).then_inc(s_token, 1)
                dve.tensor_reduce(gate[k][:, :], bank[7][:, 2:5], AX.X, ALU.add)
                dve.wait_ge(s_token, base + n)
                dve.tensor_scalar(slot[k][:, :], token[k % 2][:, :], float(FAR), binf[:, :], ALU.add, ALU.min
                                  ).then_inc(s_index, 1)

            def xg_half(base, n, b):
                dve.wait_ge(s_pxt, base + n)
                dve.tensor_copy(xgT[b][:, 0:4, :], bank[0][:, :].rearrange("p (c t) -> p c t", t=P)
                                ).then_inc(s_xgT0, 1)

            dve.wait_ge(s_np, 1)
            passes = dve.value_load(np_i[0:1, 0:1], min_val=1, max_val=PASSES)
            with dve.Fori(0, passes, 1) as r:
                one_hot(r * NOH, 1, 0, 0)
                one_hot(r * NOH, 2, 1, 1)
                index(r * NEX, 1, 0)
                index(r * NEX, 2, 1)
                one_hot(r * NOH, 3, 0, 2)
                xg_half(r * (NE + 1), 1, 0)

                def out(n, j):
                    b = (j + 1) % 2
                    dve.wait_ge(s_mm2, r * NE + n + j)
                    dve.wait_ge(s_scatter[b], r * (NE // 2 * 16) + n * 8 + (j + 1) // 2 * 16)
                    dve.tensor_copy(outrow[b][:, :], slot[(j + 3) % 4][:, :])
                    dve.tensor_copy(og[b][:, 512:DM], bank[6][:, :]).then_inc(s_out1, 1)

                def step(n, j, first=False):
                    blk = r * NE + n + (j + 1)
                    dve.wait_ge(s_silu, blk)
                    dve.scalar_tensor_tensor(out=hh, in0=bank[2][:, FF:2 * FF], scalar=gate[j][:, 0:1], in1=hs,
                                             op0=ALU.mult, op1=ALU.mult).then_inc(s_h, 1)
                    xg_half(r * (NE + 1) + n, j + 2, (j + 1) % 2)
                    index(r * NEX + n, j + 3, (j + 2) % 4)
                    if not first:
                        out(n, j)
                    one_hot(r * NOH + n, j + 4, (j + 3) % 2, n + (j + 3))

                for j in range(4):
                    step(0, j, j == 0)
                with dve.Fori(4, NE, 4) as n:
                    for j in range(4):
                        step(n, j)
                out(NE, 0)
                dve.wait_ge(s_onehot, (r + 1) * NOH)
                dve.tensor_scalar(iotap[:, :], iotap[:, :], float(P), None, ALU.add).then_inc(s_place, 1)
                dve.wait_ge(s_place, r + 1)
                for b in range(2):
                    dve.wait_ge(s_gather[b], (r + 1) * HG)
                dve.wait_ge(s_xgT0, (r + 1) * (NE + 1))

            def embed(i):
                r = ROWS[i]
                wait_drained(dve, "gt", i, 1)
                g = gsig[i % 2][0:r, :]
                link(dve.scalar_tensor_tensor(out=g, in0=g, scalar=1.0, in1=proj[0:r, i, :],
                                              op0=ALU.add, op1=ALU.mult))
                dve.scalar_tensor_tensor(out=x[0:r, i, :], in0=g, scalar=0.5, in1=x[0:r, i, :],
                                         op0=ALU.mult, op1=ALU.add).then_inc(s_x3, 1)

            def final(i):
                r = ROWS[i]
                dve.wait_ge(s_rstdf, i + 1)
                if i >= 2:
                    dve.wait_ge(s_yo[i % 2], 16 * (i // 2))
                dve.scalar_tensor_tensor(out=og[i % 2][0:r, :], in0=x[0:r, i, :], scalar=rstdf[0:r, i:i + 1],
                                         in1=g_b[0:r, :], op0=ALU.mult, op1=ALU.mult).then_inc(s_y, 1)

            dve.wait_ge(s_ga, 32)
            dve.wait_ge(s_gb, 32)
            normalise(0, xs3[0], g_a, 2 * NT)
            for i in range(NT):
                if i + 1 < NT:
                    if i:
                        after(dve, "x3T", i - 1, 1)
                    normalise(i + 1, xs3[(i + 1) % 2], g_a, 2 * NT)
                turned("x3T", i)
                if i:
                    embed(i - 1)
                if i >= 2:
                    final(i - 2)
            embed(NT - 1)
            final(NT - 2)
            final(NT - 1)

        @block.tensor
        def _(pe):
            def turn(key, i, src):
                r = ROWS[i]
                for n in range(2):
                    b = free_bank(pe, key, i, n)
                    for c in range(4):
                        s = (4 * n + c) * P
                        ins = pe.transpose(b[:, P * c:P * c + r], src[0:r, s:s + P], ident[0:r, 0:r])
                    ins.then_inc(filled, 1)

            def reduce_over(b, lhs, rhs, nk):
                for c in range(nk):
                    ins = pe.matmul(b, lhs(c), rhs(c), start=(c == 0), stop=(c == nk - 1))
                return ins

            pe.wait_ge(s_const, 2)
            for i in range(NT):
                pe.wait_ge(s_xs, i + 1)
                turn("x1T", i, xs1[:, i % 2, :])
            wait_drained(pe, "x1T", NT - 1, 0)
            wait_drained(pe, "x1T", NT - 1, 1)
            pe.wait_ge(s_wg, 32)
            for n in range(2):
                b = free_bank(pe, "g", n)
                reduce_over(b[0:36, 0:TH], lambda c: wg[:, c, :], lambda c: xT[:, c, TH * n:TH * n + TH], KT
                            ).then_inc(filled, 1)
            for name in ("q", "k", "u"):
                chunk_in(pe, name)
                w = chunk(name).rearrange("p (c n) -> p c n", n=512)
                for j in range(H):
                    for n in range(2):
                        b = free_bank(pe, name, j, n)
                        reduce_over(b[:, 0:TH], lambda c: w[:, c, P * j:P * j + P],
                                    lambda c: xT[:, c, TH * n:TH * n + TH], KT).then_inc(filled, 1)
            pe.wait_ge(s_state, 32)
            b = free_bank(pe, "buf")
            for j in range(H):
                ins = pe.transpose(b[:, P * j:P * j + NB * R], bufnat[:, P * j:P * j + P], ident[0:NB * R, 0:NB * R])
            ins.then_inc(filled, 1)

            def natural(key, i):
                b = free_bank(pe, key, i)
                w = chunk(key).rearrange("p (c n) -> p c n", n=512)
                reduce_over(b[0:ROWS[i], :], lambda c: xT[:, c, tok(i)], lambda c: w[:, c, :], KT
                            ).then_inc(filled, 1)

            chunk_in(pe, "v")
            for i in range(NT):
                natural("v", i)
            pe.wait_ge(s_em, 1)
            b = free_bank(pe, "nat")
            for a, row in enumerate((a_row, em_row)):
                for i in range(NT):
                    n0 = (a * NT + i) * H
                    ins = pe.transpose(b[0:ROWS[i], n0:n0 + H], row[:, tok(i)], ident[0:H, 0:H])
            ins.then_inc(filled, 1)
            for j in range(H):
                pe.wait_ge(s_pooled, j + 1)
                for n in range(2):
                    b = free_bank(pe, "mix", j, n)
                    pe.matmul(b[:, 0:TH], wp[:, j, :], pooled[:, j % 2, TH * n:TH * n + TH], start=True, stop=True
                              ).then_inc(filled, 1)
            b = free_bank(pe, "pp")
            for j in range(H):
                ins = pe.transpose(b[0:R, P * j:P * j + P], uext[:, j, SEQ:SEGP], ident[:, :])
            ins.then_inc(filled, 1)
            b = free_bank(pe, "ps")
            for j in range(H):
                ins = pe.transpose(b[0:NS, P * j:P * j + P],
                                   us[:, j, :], ident[:, :])
            ins.then_inc(filled, 1)
            chunk_in(pe, "o")
            wait_drained(pe, "k", H - 1, 1)
            for h in range(H):
                b = free_bank(pe, "Mb", h)
                pe.matmul(b[:, :], sel4[:, h, :], M_row[:, 0:SEQ], start=True, stop=True).then_inc(filled, 1)
                for j in range(NP_):
                    b = free_bank(pe, "S", h, j)
                    pe.matmul(b[:, 0:SEQ - P * j], kT[:, h, P * j:P * j + P], qT[:, h, P * j:SEQ], start=True,
                              stop=True).then_inc(filled, 1)
                natural("o", h)
                wait_drained(pe, "S", h, NP_ - 1)
                for i in range(NP_):
                    b = free_bank(pe, "num", h, i)
                    for j in range(i + 1):
                        at = BLK[j] + P * (i - j)
                        ins = pe.matmul(b[:, 0:DE], PT[:, at:at + P], v[:, j, h, :], start=(j == 0), stop=(j == i))
                    ins.then_inc(filled, 1)
            W = 2 * NS + NB
            for k in range(2):
                b = free_bank(pe, "Ms", k)
                for h in (2 * k, 2 * k + 1):
                    ins = pe.matmul(b[:, W * (h % 2):W * (h % 2 + 1)], sel4[:, h, :], srow, start=True, stop=True)
                ins.then_inc(filled, 1)
            b = free_bank(pe, "Ss")
            for h in range(H):
                ins = pe.matmul(b[0:NS, NS * h:NS * h + NS], kT[:, h, SEQ:T], qT[:, h, SEQ:T], start=True, stop=True)
            ins.then_inc(filled, 1)
            for h in range(H):
                b = free_bank(pe, "kn", h)
                for j in range(NP_):
                    ins = pe.transpose(b[:, P * j:P * j + P], kT[:, h, P * j:P * j + P], ident[:, :])
                ins.then_inc(filled, 1)
                wait_drained(pe, "kn", h)
                b = free_bank(pe, "Cp", h)
                reduce_over(b[:, 0:DE], lambda c: kw[:, h % 2, c, :], lambda c: v[:, c, h, :], NP_).then_inc(filled, 1)
            b = free_bank(pe, "kns")
            for h in range(H):
                ins = pe.transpose(b[0:NS, P * h:P * h + P], kT[:, h, SEQ:T], ident[:, :])
            ins.then_inc(filled, 1)
            pe.wait_ge(s_c0, 16 * (NB + 1))
            b = free_bank(pe, "n0")
            pe.transpose(b[:, 0:NB * H], n0nat, ident[0:NB * H, 0:NB * H]).then_inc(filled, 1)
            natural("o", 4)
            wait_drained(pe, "Ss")
            wait_drained(pe, "n0")
            b = free_bank(pe, "nT")
            for h in range(H):
                pe.matmul(b[:, NS * h:NS * h + NS], v[0:NS, NP_, h, 0:P], PTs[:, h, :], start=True, stop=False,
                          skip_group_check=True)
                for k in range(NB):
                    c = NS * h + DS * k
                    ins = pe.matmul(b[:, c:c + DS], C0[:, k, h, 0:P], qw[:, h, DS * k:DS * k + DS], start=False,
                                    stop=(k == NB - 1), skip_group_check=True)
            ins.then_inc(filled, 1)
            b = free_bank(pe, "nqs")
            for h in range(H):
                pe.matmul(b[0:NS, 16 * h:16 * h + NB], qw[:, h, :], C0[:, :, h, P], start=True, stop=True)
                ins = pe.matmul(b[0:NS, 16 * h + NB:16 * h + NB + 1], PTs[:, h, :], onesf[0:NS, 0:1], start=True,
                                stop=True)
            ins.then_inc(filled, 1)
            wait_drained(pe, "nT")
            b = free_bank(pe, "nTt")
            for h in range(H):
                ins = pe.transpose(b[0:NS, P * h:P * h + P], numT[:, h, :], ident[:, :])
            ins.then_inc(filled, 1)
            wait_drained(pe, "kns")
            for h in range(H):
                pe.wait_ge(s_vb, h + 1)
                for c in range(3):
                    nb_ = min(3, NB - 3 * c)
                    b = free_bank(pe, "C", h, c)
                    pe.matmul(b[:, 0:nb_ * DE], kws[:, h, :], Vb[0:NS, 3 * c:3 * c + nb_, :], start=True, stop=True
                              ).then_inc(filled, 1)
            for i in range(NT):
                pe.wait_ge(s_ha, i + 1)
                b = free_bank(pe, "haT", i)
                r = ROWS[i]
                for h in range(H):
                    ins = pe.transpose(b[:, P * h:P * h + r], ha[0:r, i % 2, P * h:P * h + P], ident[0:r, 0:r])
                ins.then_inc(filled, 1)
            wait_drained(pe, "Cp", H - 1)
            b = free_bank(pe, "nout")
            pe.transpose(b[0:NB * H, 0:P], C0[:, :, :, P].rearrange("p b h -> p (b h)"), ident[:, :])
            pe.transpose(b[0:H, P:2 * P], Cp[:, :, P], ident[:, :]).then_inc(filled, 1)

            def wo(i):
                for n in range(2):
                    chunk_in(pe, f"wo{n}")
                    b = free_bank(pe, "wo", i, n)
                    w = chunk(f"wo{n}").rearrange("p (c n) -> p c n", n=512)
                    reduce_over(b[0:ROWS[i], :], lambda c: mixT[:, c, tok(i)], lambda c: w[:, c, :], KT
                                ).then_inc(filled, 1)

            def norm2(i):
                r = ROWS[i]
                pe.wait_ge(s_xs, NT + i + 1)
                turn("x2T", i, xs2[i % 2])
                wait_drained(pe, "x2T", i, 0)
                wait_drained(pe, "x2T", i, 1)
                b = free_bank(pe, "r", i)
                reduce_over(b[0:r, 0:NE], lambda c: xT[:, c, tok(i)], lambda c: rw[:, c, :], KT).then_inc(filled, 1)
                b = free_bank(pe, "sh", i)
                reduce_over(b[0:r, :], lambda c: xT[:, c, tok(i)], lambda c: w13[1][:, :, c, :], KT
                            ).then_inc(filled, 1)

            def shared(i):
                r = ROWS[i]
                pe.wait_ge(s_hsh, i + 1)
                b = free_bank(pe, "shT", i)
                for c in range(2):
                    ins = pe.transpose(b[:, P * c:P * c + r], hh[0:r, P * c:P * c + P], ident[0:r, 0:r])
                ins.then_inc(filled, 1)
                wait_drained(pe, "shT", i)
                for n in range(2):
                    b = free_bank(pe, "y", i, n)
                    reduce_over(b[0:r, :], lambda c: hT[:, c, 0:r], lambda c: w2s[1][:, c, 512 * n:512 * n + 512], 2
                                ).then_inc(filled, 1)

            wait_drained(pe, "haT", NT - 1)
            wo(0)
            wo(1)
            pe.wait_ge(s_rt, 32)
            pe.wait_ge(s_sh, 48)
            norm2(0)
            wo(2)
            shared(0)
            norm2(1)
            wo(3)
            shared(1)
            norm2(2)
            wo(4)
            shared(2)
            norm2(3)
            pe.wait_ge(s_p, 16 * NT)
            for i in range(NT):
                r = ROWS[i]
                b = free_bank(pe, "pT", i)
                for c in range(2):
                    ins = pe.transpose(b[:, P * c:P * c + r], ptile[0:r, i, P * c:P * c + P], ident[0:r, 0:r])
                ins.then_inc(filled, 1)
            shared(3)
            norm2(4)

            def pj(i):
                r = ROWS[i]
                w = chunk("pj")[:, 0:2 * DM].rearrange("p (c n) -> p c n", n=DM)
                for n in range(2):
                    b = free_bank(pe, "pj", i, n)
                    reduce_over(b[0:r, :], lambda c: pT[:, c, tok(i)], lambda c: w[:, c, 512 * n:512 * n + 512], 2
                                ).then_inc(filled, 1)

            chunk_in(pe, "pj")
            wait_drained(pe, "pT", NT - 1)
            pj(0)
            pj(1)
            shared(4)
            for i in range(2, NT):
                pj(i)
            pe.wait_ge(s_sel0, 1)
            b = free_bank(pe, "pos")
            for i in range(NT + 1):
                for k in range(min(i + 1, NT)):
                    ins = pe.matmul(b[:, NE * i:NE * i + NE], before[:, :] if k == i else onesf[:, :], sel_[:, k, :],
                                    start=(k == 0), stop=(k == min(i, NT - 1)))
            ins.then_inc(filled, 1)

            def pick(r, n, m, b):
                pe.wait_ge(s_onehot, r * NOH + n + m)
                for i in range(NT):
                    ins = pe.matmul(bank[7][:, 0:5], onehot[b][:, i, :], pick6[b][:, i, 0:5], start=(i == 0),
                                    stop=(i == NT - 1))
                ins.then_inc(s_psel, 1)

            def turn_rows(gathers, b):
                pe.wait_ge(s_gather[b], gathers)
                for c in range(8):
                    ins = pe.transpose(bank[c // 4][:, P * (c % 4):P * (c % 4) + P], xg[b][:, P * c:P * c + P],
                                       ident[:, :])
                ins.then_inc(s_pxt, 1)

            wait_drained(pe, "pos")
            wait_drained(pe, "pj", NT - 1, 1)
            pe.wait_ge(s_np, 1)
            passes = pe.value_load(np_i[0:1, 0:1], min_val=1, max_val=PASSES)
            with pe.Fori(0, passes, 1) as r:
                pick(r, 0, 1, 0)
                pe.wait_ge(s_index, r * NEX + 1)
                pick(r, 0, 2, 1)
                turn_rows(r * HG + 16, 0)

                def mm2(n, j):
                    b = (j + 1) % 2
                    pe.wait_ge(s_hT, r * NE + n + j)
                    pe.wait_ge(s_w2[b], r * (NE // 2 * 16) + n * 8 + (j + 1) // 2 * 16)
                    for half in range(2):
                        for c in range(2):
                            ins = pe.matmul(bank[5 + half][:, :], hT[:, c, :],
                                            w2s[b][:, c, 512 * half:512 * half + 512], start=(c == 0),
                                            stop=(c == 1))
                    ins.then_inc(s_mm2, 1)

                def step(n, j, first=False):
                    b = j % 2
                    pe.wait_ge(s_w13[b], r * (NE // 2 * 32) + n * 16 + (j // 2 + 1) * 32)
                    pe.wait_ge(s_xgT0, r * (NE + 1) + n + (j + 1))
                    pe.wait_ge(s_xgT1, r * (NE + 1) + n + (j + 1))
                    for c in range(KT):
                        ins = pe.matmul(bank[2][:, :], xgT[b][:, c, :], w13[b][:, :, c, :], start=(c == 0),
                                        stop=(c == KT - 1))
                    ins.then_inc(s_mm1, 1)
                    turn_rows(r * HG + n * 8 + (16 if j < 1 else 32 if j < 3 else 48), 1 - b)
                    pe.wait_ge(s_index, r * NEX + n + (j + 2))
                    pick(r, n, j + 3, b)
                    if not first:
                        mm2(n, j)
                    pe.wait_ge(s_h, r * NE + n + (j + 1))
                    for c in range(2):
                        ins = pe.transpose(bank[4][:, P * c:P * c + P], hh[:, P * c:P * c + P], ident[:, :])
                    ins.then_inc(s_pht, 1)

                for j in range(4):
                    step(0, j, j == 0)
                with pe.Fori(4, NE, 4) as n:
                    for j in range(4):
                        step(n, j)
                pe.wait_ge(s_out1, r * NE + (NE - 1))
                mm2(NE, 0)
            pe.wait_ge(s_out0, passes * NE)
            pe.wait_ge(s_out1, passes * NE)
            pe.wait_ge(s_xgT0, passes * (NE + 1))
            pe.wait_ge(s_xgT1, passes * (NE + 1))
            pe.wait_ge(s_index, passes * NEX)

            for i in range(NT + 1):
                if i < NT:
                    pe.wait_ge(s_xs, 2 * NT + i + 1)
                    turn("x3T", i, xs3[i % 2])
                if i == 0:
                    continue
                i -= 1
                r = ROWS[i]
                wait_drained(pe, "x3T", i, 0)
                wait_drained(pe, "x3T", i, 1)
                for n in range(2):
                    chunk_in(pe, f"gt{n}")
                    b = free_bank(pe, "gt", i, n)
                    w = chunk(f"gt{n}").rearrange("p (c n) -> p c n", n=512)
                    reduce_over(b[0:r, :], lambda c: xT[:, c, tok(i)], lambda c: w[:, c, :], KT
                                ).then_inc(filled, 1)


_INS = ["x_prompt", "x_sample", "p_prompt", "p_sample", "state_C", "state_n", "state_m", "state_pool",
        "norm_mix_g", "w_in", "b_igate", "b_fgate", "head_norm_g", "w_pool", "pool_scale", "w_out",
        "norm_ffn_g", "router_w", "router_bias", "ex_w1", "ex_w3", "ex_w2", "sh_w1", "sh_w3", "sh_w2",
        "norm_ple_g", "w_ple_gate", "w_ple_proj", "final_norm_g"]
_OUTS = ["y_prompt", "y_sample", "C_prompt", "n_prompt", "m_prompt", "pool_prompt",
         "C_sample", "n_sample", "m_sample", "pool_sample"]


def kernel(**inputs):
    import numpy as _np
    import concourse.bacc as _bacc
    from concourse import mybir as _mybir
    from concourse.bass_utils import run_bass_kernel_spmd as _run

    nc = _bacc.Bacc("TRN2", target_bir_lowering=False, num_devices=1)
    arrays, args = {}, []
    for name in _INS:
        a = _np.ascontiguousarray(inputs[name])
        arrays[f"in_{name}"] = a
        args.append(nc.dram_tensor(f"in_{name}", a.shape, _mybir.dt.from_np(a.dtype), kind="ExternalInput").ap())
    depth, batch = inputs["p_prompt"].shape[:2]
    heads, dh = inputs["state_n"].shape[2:]
    rows, width = inputs["state_pool"].shape[2:]
    nb = inputs["x_sample"].shape[0]
    shapes = [inputs["x_prompt"].shape, inputs["x_sample"].shape]
    for b in (batch, nb):
        shapes += [(depth, b, heads, dh, dh), (depth, b, heads, dh), (depth, b, heads), (depth, b, rows, width)]
    for name, shape in zip(_OUTS, shapes):
        args.append(nc.dram_tensor(f"out_{name}", shape, _mybir.dt.float32, kind="ExternalOutput").ap())
    decoder_step(nc, *args)
    r = _run(nc, [arrays], core_ids=[0])
    return tuple(r.results[0][f"out_{name}"] for name in _OUTS)
```
